# Optimizing a Trainium2 kernel written in Bass

```python
import numpy as np
import jax
import jax.numpy as jnp
from jax import lax

D_MODEL = 1024
BATCH = 1
SEQ = 512
DEPTH = 2

N_BRANCH = 4
BRANCH_WIDTH = 512
CONV_TAPS = 3
SC_WIDTH = BRANCH_WIDTH
NSA_HEADS = 8
NSA_KV_GROUPS = 2
NSA_HPG = NSA_HEADS // NSA_KV_GROUPS
NSA_HEAD_DIM = BRANCH_WIDTH // NSA_HEADS
CMP_BLOCK = 32
CMP_STRIDE = 16
SEL_BLOCK = 64
SEL_TOP_N = 16
SEL_Q_CHUNK = 32
WINDOW = 512
WIN_Q_BLOCK = 128
ROPE_THETA = 500000.0
ROPE_DIM = NSA_HEAD_DIM // 4
FORCE_SCORE = 1.0e4
RET_HEADS = 4
RET_HEAD_DIM = BRANCH_WIDTH // RET_HEADS
RET_CHUNK = 128
RET_THETA = 10000.0
POOL_WINDOWS = (2, 4, 8, 16)
POOL_GROUPS = 4
POOL_GROUP_DIM = BRANCH_WIDTH // POOL_GROUPS
D_FF = 2816
EPS = 1e-6
NEG_INF = -1e30

IN_SPLITS = (3 * SC_WIDTH, NSA_HEADS * NSA_HEAD_DIM, 3 * 2 * NSA_KV_GROUPS * NSA_HEAD_DIM, 3 * NSA_HEADS, 4 * BRANCH_WIDTH, BRANCH_WIDTH, N_BRANCH * D_MODEL)
D_IN = sum(IN_SPLITS)

kernel_name = 'hybrid_gated_parallel_mixer'

def rms_norm(x, g):
    x32 = x.astype(jnp.float32)
    y = x32 * lax.rsqrt(jnp.mean(x32 * x32, axis=-1, keepdims=True) + EPS)
    return (y * g.astype(jnp.float32)).astype(x.dtype)

def rotary(x, pos, rot_dim, theta):
    half = rot_dim // 2
    inv_freq = np.power(np.float32(theta), -np.arange(half, dtype=np.float32) / np.float32(half))
    ang = pos.astype(jnp.float32)[:, None] * jnp.asarray(inv_freq)[None, :]
    cos = jnp.cos(ang)[:, None, :].astype(x.dtype)
    sin = jnp.sin(ang)[:, None, :].astype(x.dtype)
    x1 = x[..., :half]
    x2 = x[..., half:rot_dim]
    return jnp.concatenate([x1 * cos - x2 * sin, x2 * cos + x1 * sin, x[..., rot_dim:]], axis=-1)

def causal_dwconv(x, w):
    k_taps, ch = w.shape
    return lax.conv_general_dilated(x, w[:, None, :], window_strides=(1,), padding=((k_taps - 1, 0),), dimension_numbers=('NWC', 'WIO', 'NWC'), feature_group_count=ch)

def masked_softmax(s, mask):
    return jax.nn.softmax(jnp.where(mask, s.astype(jnp.float32), NEG_INF), axis=-1)

def short_conv_mixer(z, conv_w):
    b, c, h = jnp.split(z, 3, axis=-1)
    return b * causal_dwconv(c * h, conv_w)

def nsa_mixer(zq, zkv, zg, cmp_pe, cmp_w1_k, cmp_w2_k, cmp_w1_v, cmp_w2_v):
    B, S, _ = zq.shape
    G, J, Dh = NSA_KV_GROUPS, NSA_HPG, NSA_HEAD_DIM
    pos = jnp.arange(S)
    q = rotary(zq.reshape(B, S, NSA_HEADS, Dh), pos, ROPE_DIM, ROPE_THETA) * (Dh ** -0.5)
    q = q.reshape(B, S, G, J, Dh)
    kv = zkv.reshape(B, S, 3, 2, G, Dh)
    k_cmp, v_cmp = kv[:, :, 0, 0], kv[:, :, 0, 1]
    k_slc, v_slc = rotary(kv[:, :, 1, 0], pos, ROPE_DIM, ROPE_THETA), kv[:, :, 1, 1]
    k_win, v_win = rotary(kv[:, :, 2, 0], pos, ROPE_DIM, ROPE_THETA), kv[:, :, 2, 1]

    n_cmp = (S - CMP_BLOCK) // CMP_STRIDE + 1
    blk = np.arange(n_cmp)[:, None] * CMP_STRIDE + np.arange(CMP_BLOCK)[None, :]
    cmp_end = jnp.asarray(np.arange(n_cmp) * CMP_STRIDE + CMP_BLOCK - 1)

    def compress(t, w1, w2):
        tb = t[:, blk] + cmp_pe[None, None, :, None, :]
        hid = jax.nn.gelu(jnp.einsum('bnlgd,lde->bnge', tb, w1))
        return jnp.einsum('bnge,ef->bngf', hid, w2)

    k_c = rotary(compress(k_cmp, cmp_w1_k, cmp_w2_k), cmp_end, ROPE_DIM, ROPE_THETA)
    v_c = compress(v_cmp, cmp_w1_v, cmp_w2_v)
    mask_c = cmp_end[None, :] <= pos[:, None]
    s_c = jnp.einsum('bsgjd,bngd->bgjsn', q, k_c)
    p_c = masked_softmax(s_c, mask_c) * mask_c
    o_cmp = jnp.einsum('bgjsn,bngd->bsgjd', p_c.astype(v_c.dtype), v_c)

    n_sel = S // SEL_BLOCK
    cs0 = np.arange(n_cmp) * CMP_STRIDE
    ss0 = np.arange(n_sel) * SEL_BLOCK
    overlap = np.clip(np.minimum(cs0[:, None] + CMP_BLOCK, ss0[None, :] + SEL_BLOCK) - np.maximum(cs0[:, None], ss0[None, :]), 0, None)
    overlap = jnp.asarray((overlap / CMP_BLOCK).astype(np.float32))
    imp = jnp.einsum('bgjsn,nm->bgsm', p_c, overlap)
    cur = pos // SEL_BLOCK
    bid = jnp.arange(n_sel)
    forced = (bid[None, :] == 0) | (bid[None, :] == cur[:, None]) | (bid[None, :] == cur[:, None] - 1)
    future = bid[None, :] > cur[:, None]
    imp = jnp.where(forced, FORCE_SCORE, jnp.where(future, -FORCE_SCORE, imp))
    n_top = min(SEL_TOP_N, n_sel)
    _, sel_idx = lax.top_k(imp, n_top)

    k_blocks = k_slc.reshape(B, n_sel, SEL_BLOCK, G, Dh).transpose(0, 3, 1, 2, 4)
    v_blocks = v_slc.reshape(B, n_sel, SEL_BLOCK, G, Dh).transpose(0, 3, 1, 2, 4)
    n_qc = S // SEL_Q_CHUNK
    q_ch = q.reshape(B, n_qc, SEL_Q_CHUNK, G, J, Dh).swapaxes(0, 1)
    idx_ch = sel_idx.reshape(B, G, n_qc, SEL_Q_CHUNK, n_top).transpose(2, 0, 1, 3, 4)
    t_ch = pos.reshape(n_qc, SEL_Q_CHUNK)
    b_i = jnp.arange(B)[:, None, None, None]
    g_i = jnp.arange(G)[None, :, None, None]

    def sel_chunk(args):
        qc, ic, tc = args
        kg = k_blocks[b_i, g_i, ic]
        vg = v_blocks[b_i, g_i, ic]
        kpos = ic[..., None] * SEL_BLOCK + jnp.arange(SEL_BLOCK)
        m = (kpos <= tc[None, None, :, None, None]).reshape(B, G, 1, SEL_Q_CHUNK, n_top * SEL_BLOCK)
        s = jnp.einsum('bqgjd,bgqkld->bgjqkl', qc, kg).reshape(B, G, J, SEL_Q_CHUNK, n_top * SEL_BLOCK)
        p = masked_softmax(s, m).astype(vg.dtype).reshape(B, G, J, SEL_Q_CHUNK, n_top, SEL_BLOCK)
        return jnp.einsum('bgjqkl,bgqkld->bqgjd', p, vg)

    o_slc = lax.map(sel_chunk, (q_ch, idx_ch, t_ch)).swapaxes(0, 1).reshape(B, S, G, J, Dh)

    n_wb = S // WIN_Q_BLOCK
    span = WINDOW + WIN_Q_BLOCK
    k_pad = jnp.pad(k_win, ((0, 0), (WINDOW, 0), (0, 0), (0, 0)))
    v_pad = jnp.pad(v_win, ((0, 0), (WINDOW, 0), (0, 0), (0, 0)))
    q_wb = q.reshape(B, n_wb, WIN_Q_BLOCK, G, J, Dh).swapaxes(0, 1)

    def win_block(args):
        qb, c = args
        start = c * WIN_Q_BLOCK
        kb = lax.dynamic_slice_in_dim(k_pad, start, span, axis=1)
        vb = lax.dynamic_slice_in_dim(v_pad, start, span, axis=1)
        tq = start + jnp.arange(WIN_Q_BLOCK)
        tk = start - WINDOW + jnp.arange(span)
        m = (tk[None, :] <= tq[:, None]) & (tk[None, :] > tq[:, None] - WINDOW) & (tk[None, :] >= 0)
        s = jnp.einsum('bqgjd,bkgd->bgjqk', qb, kb)
        p = masked_softmax(s, m).astype(vb.dtype)
        return jnp.einsum('bgjqk,bkgd->bqgjd', p, vb)

    o_win = lax.map(win_block, (q_wb, jnp.arange(n_wb))).swapaxes(0, 1).reshape(B, S, G, J, Dh)

    g = jax.nn.sigmoid(zg.reshape(B, S, G, J, 3))
    o = g[..., 0:1] * o_cmp + g[..., 1:2] * o_slc + g[..., 2:3] * o_win
    return o.reshape(B, S, NSA_HEADS * Dh)

def retention_mixer(z, gn_g):
    B, S, _ = z.shape
    H, dk, C = RET_HEADS, RET_HEAD_DIM, RET_CHUNK
    zq, zk, zv, zg = jnp.split(z, 4, axis=-1)
    pos = jnp.arange(S)
    q = rotary(zq.reshape(B, S, H, dk), pos, dk, RET_THETA).astype(jnp.float32)
    k = rotary(zk.reshape(B, S, H, dk), pos, dk, RET_THETA).astype(jnp.float32) * (dk ** -0.5)
    v = zv.reshape(B, S, H, dk).astype(jnp.float32)
    n_c = S // C

    def to_chunks(t):
        return t.reshape(B, n_c, C, H, dk).transpose(1, 0, 3, 2, 4)

    log_g = np.log1p(-np.exp2(-5.0 - np.arange(H))).astype(np.float32)
    n = np.arange(C, dtype=np.float32)
    diff = n[:, None] - n[None, :]
    intra = jnp.asarray(np.where(diff >= 0, np.exp(np.maximum(diff, 0.0)[None] * log_g[:, None, None]), 0.0).astype(np.float32))
    q_dec = jnp.asarray(np.exp((n[None, :] + 1.0) * log_g[:, None]).astype(np.float32))
    k_dec = jnp.asarray(np.exp((C - 1.0 - n[None, :]) * log_g[:, None]).astype(np.float32))
    c_dec = jnp.asarray(np.exp(C * log_g).astype(np.float32))

    def step(R, inp):
        qc, kc, vc = inp
        scores = jnp.einsum('bhnd,bhmd->bhnm', qc, kc) * intra
        inner = jnp.einsum('bhnm,bhme->bhne', scores, vc)
        cross = jnp.einsum('bhnd,bhde->bhne', qc * q_dec[:, :, None], R)
        R = R * c_dec[:, None, None] + jnp.einsum('bhmd,bhme->bhde', kc * k_dec[:, :, None], vc)
        return R, inner + cross

    R0 = jnp.zeros((B, H, dk, dk), jnp.float32)
    _, o = lax.scan(step, R0, (to_chunks(q), to_chunks(k), to_chunks(v)))
    o = o.transpose(1, 0, 3, 2, 4).reshape(B, S, H, dk)
    mu = jnp.mean(o, axis=-1, keepdims=True)
    var = jnp.mean(jnp.square(o - mu), axis=-1, keepdims=True)
    o = ((o - mu) * lax.rsqrt(var + EPS)).reshape(B, S, H * dk) * gn_g.astype(jnp.float32)
    return (o * jax.nn.silu(zg.astype(jnp.float32))).astype(z.dtype)

def pool_mixer(u, pool_w, pool_scale):
    B, S, _ = u.shape
    ug = u.reshape(B, S, POOL_GROUPS, POOL_GROUP_DIM).astype(jnp.float32)
    cs = jnp.pad(jnp.cumsum(ug, axis=1), ((0, 0), (1, 0), (0, 0), (0, 0)))
    t = np.arange(S)
    win = np.array(POOL_WINDOWS)
    lo = np.maximum(t[:, None] + 1 - win[None, :], 0)
    cnt = jnp.asarray((t[:, None] + 1 - lo).astype(np.float32))
    win_sum = cs[:, 1:] - cs[:, lo, np.arange(POOL_GROUPS)[None, :]]
    pooled = (win_sum / cnt[None, :, :, None] - ug).astype(u.dtype)
    y = jnp.einsum('bsgc,gcd->bsgd', pooled, pool_w).reshape(B, S, BRANCH_WIDTH)
    return y * pool_scale

def hybrid_layer(x, norm1_g, w_in, b_gate, sc_conv, cmp_pe, cmp_w1_k, cmp_w2_k, cmp_w1_v, cmp_w2_v, ret_gn_g, pool_w, pool_scale, w_branch, w_o, norm2_g, w_up, ffn_conv, w_down):
    B, S, D = x.shape
    h = rms_norm(x, norm1_g)
    z = h @ w_in
    z_sc, z_q, z_kv, z_ng, z_ret, z_pool, z_gate = jnp.split(z, np.cumsum(IN_SPLITS)[:-1].tolist(), axis=-1)
    y_a = short_conv_mixer(z_sc, sc_conv)
    y_b = nsa_mixer(z_q, z_kv, z_ng, cmp_pe, cmp_w1_k, cmp_w2_k, cmp_w1_v, cmp_w2_v)
    y_c = retention_mixer(z_ret, ret_gn_g)
    y_d = pool_mixer(z_pool, pool_w, pool_scale)
    branches = jnp.stack([y_a, y_b, y_c, y_d], axis=2)
    gates = jax.nn.sigmoid((z_gate + b_gate).reshape(B, S, N_BRANCH, D))
    merged = jnp.sum(jnp.einsum('bsnc,ncd->bsnd', branches, w_branch) * gates, axis=2)
    x = x + merged @ w_o
    h = rms_norm(x, norm2_g)
    u_gate, u_val = jnp.split(h @ w_up, 2, axis=-1)
    return x + (jax.nn.silu(causal_dwconv(u_gate, ffn_conv)) * u_val) @ w_down

def setup_inputs(seed: int = 0) -> dict:
    key = jax.random.key(seed)
    ks = jax.random.split(key, 21)
    f32 = jnp.float32
    Dh = NSA_HEAD_DIM

    def nrm(k, shape, scale):
        return jax.random.normal(k, shape, f32) * scale

    def gain(k, shape):
        return 1.0 + 0.02 * jax.random.normal(k, shape, f32)

    return {
        'x': nrm(ks[0], (BATCH, SEQ, D_MODEL), 1.0),
        'norm1_g': gain(ks[1], (DEPTH, D_MODEL)),
        'w_in': nrm(ks[2], (DEPTH, D_MODEL, D_IN), D_MODEL ** -0.5),
        'b_gate': nrm(ks[3], (DEPTH, N_BRANCH * D_MODEL), 0.02),
        'sc_conv': nrm(ks[4], (DEPTH, CONV_TAPS, SC_WIDTH), CONV_TAPS ** -0.5),
        'cmp_pe': nrm(ks[5], (DEPTH, CMP_BLOCK, Dh), 0.1),
        'cmp_w1_k': nrm(ks[6], (DEPTH, CMP_BLOCK, Dh, Dh), (CMP_BLOCK * Dh) ** -0.5),
        'cmp_w2_k': nrm(ks[7], (DEPTH, Dh, Dh), Dh ** -0.5),
        'cmp_w1_v': nrm(ks[8], (DEPTH, CMP_BLOCK, Dh, Dh), (CMP_BLOCK * Dh) ** -0.5),
        'cmp_w2_v': nrm(ks[9], (DEPTH, Dh, Dh), Dh ** -0.5),
        'ret_gn_g': gain(ks[10], (DEPTH, BRANCH_WIDTH)),
        'pool_w': nrm(ks[11], (DEPTH, POOL_GROUPS, POOL_GROUP_DIM, POOL_GROUP_DIM), POOL_GROUP_DIM ** -0.5),
        'pool_scale': gain(ks[12], (DEPTH, BRANCH_WIDTH)),
        'w_branch': nrm(ks[13], (DEPTH, N_BRANCH, BRANCH_WIDTH, D_MODEL), BRANCH_WIDTH ** -0.5),
        'w_o': nrm(ks[14], (DEPTH, D_MODEL, D_MODEL), D_MODEL ** -0.5),
        'norm2_g': gain(ks[15], (DEPTH, D_MODEL)),
        'w_up': nrm(ks[16], (DEPTH, D_MODEL, 2 * D_FF), D_MODEL ** -0.5),
        'ffn_conv': nrm(ks[17], (DEPTH, CONV_TAPS, D_FF), CONV_TAPS ** -0.5),
        'w_down': nrm(ks[18], (DEPTH, D_FF, D_MODEL), D_FF ** -0.5),
        'final_norm_g': gain(ks[19], (D_MODEL,)),
    }

def reference(x, norm1_g, w_in, b_gate, sc_conv, cmp_pe, cmp_w1_k, cmp_w2_k, cmp_w1_v, cmp_w2_v, ret_gn_g, pool_w, pool_scale, w_branch, w_o, norm2_g, w_up, ffn_conv, w_down, final_norm_g):
    for l in range(DEPTH):
        x = hybrid_layer(x, norm1_g[l], w_in[l], b_gate[l], sc_conv[l], cmp_pe[l], cmp_w1_k[l], cmp_w2_k[l], cmp_w1_v[l], cmp_w2_v[l], ret_gn_g[l], pool_w[l], pool_scale[l], w_branch[l], w_o[l], norm2_g[l], w_up[l], ffn_conv[l], w_down[l])
    return rms_norm(x, final_norm_g)


_drawn_inputs = setup_inputs


def setup_inputs(seed=0):
    import zlib

    import numpy as np

    out = dict(_drawn_inputs(seed))
    spreads = {}
    factors = {'b_gate': 7.152,
     'ret_gn_g': 7.104,
     'pool_scale': 4.795,
     'norm2_g': 2.95,
     'final_norm_g': 8.054,
     'cmp_pe': 5.866,
     'cmp_w1_k': 3.63,
     'cmp_w2_k': 3.745}
    for name, (base, spread) in spreads.items():
        noise = np.random.default_rng([zlib.crc32(name.encode()), seed]).standard_normal(out[name].shape)
        drawn = base * np.exp(spread * noise) if base else spread * noise
        out[name] = jnp.asarray(drawn.astype(out[name].dtype))
    for name, factor in factors.items():
        out[name] = (out[name] * factor).astype(out[name].dtype)
    return out
```

```python
from contextlib import ExitStack

import numpy as np

import concourse.bass as bass
from concourse import mybir

F32 = mybir.dt.float32
F32R = mybir.dt.float32r
ALU = mybir.AluOpType
ACT = mybir.ActivationFunctionType
AX = mybir.AxisListType

P = 128
S = 512
D = 1024
DC = D // P
LAYERS = 2
BW = 512
BC = BW // P
FF = 2816
FC = FF // P
HEADS, KV_GROUPS, DH = 8, 2, 64
BLOCK, STRIDE = 32, 16
NCMP = (S - BLOCK) // STRIDE + 1
RH, RD = 4, 128
POOLS = (2, 4, 8, 16)
EPS = 1e-6
NEG = -1e30
QT = S // P

CH = 8
RING = 3
A_GROUPS = 12
B_GROUPS = 32
J_GROUPS = 6
J0 = A_GROUPS + B_GROUPS
O0 = J0 + DC * J_GROUPS
U0 = O0 + DC
D0 = U0 + 2 * FC
DG = 3
GROUPS = D0 + DC * DG
assert GROUPS % RING == 0 and J_GROUPS % RING == 0
TJ0 = J0
TO0 = TJ0 + DC * 8
TU0 = TO0 + DC
TD0 = TU0 + 2 * FC
TILES = TD0 + DC
assert TILES % 2 == 0

A_TILES = ["k_cmp", "v_cmp", "k_slc", "k_win", "v_slc", "v_win", "q0", "q1", "q2", "q3", "gate", "pad"]
RET0 = [0, 16, 20, 24]
SC0 = [4, 7, 10, 29]
POOL0 = [13, 14, 15, 28]
POOL_SLOT = [79, 95, 111, 127]
B_TILES = [None] * B_GROUPS
for _h in range(RH):
    B_TILES[RET0[_h]:RET0[_h] + 4] = [("rq", _h), ("rk", _h), ("rv", _h), ("rg", _h)]
for _j in range(BC):
    B_TILES[SC0[_j]:SC0[_j] + 3] = [("c", _j), ("h", _j), ("b", _j)]
    B_TILES[POOL0[_j]] = ("u", _j)

UNITS = 2 * QT * HEADS
SLOTS = 4 * B_GROUPS
SIDE = [[] for _ in range(SLOTS)]
for _n in range(UNITS + 7):
    _e, _qi = SIDE[_n], _n // 16
    if _n % 2 == 0 and _n < UNITS:
        _e += [("scores", _n), ("scores", _n + 1)]
    if _n % 2 and 3 <= _n <= UNITS + 1:
        _e += [("values", _n - 3), ("values", _n - 2)]
    if _n % 2 and _n < UNITS:
        _e += [("turn", _n - 1), ("turn", _n)]
    if _n < UNITS and _n % 16 == 1:
        _e.append(("cmp_scores", _qi))
    if _n < UNITS and _n % 16 == 4:
        _e.append(("cmp_turn", _qi))
    if _n >= 22 and _n % 16 == 6:
        _e.append(("mix_turn", _qi - 1))
    if _n < UNITS and _n % 16 == 7:
        _e.append(("cmp_values", _qi))
for _h in range(RH):
    _n0 = 4 * (16 + 4 * _h)
    SIDE[4 * (RET0[_h] + 3) + 2].append(("ret_turn", _h))
    for _m in range(QT):
        SIDE[_n0 + _m].append(("ret_scores", _h, _m))
        SIDE[_n0 + _m + 1].append(("ret_values", _h, _m))
    SIDE[_n0 + 5].append(("ret_gate", _h))
    SIDE[_n0 + 6].append(("ret_var", _h))
    SIDE[_n0 + 8].append(("ret_end", _h))
    SIDE[POOL_SLOT[_h]].append(("pool", _h))
SIDE[2].append(("gate",))
for _b in range(B_GROUPS - 1):
    for _k in range(4):
        if B_TILES[_b][0] == "b":
            SIDE[4 * (_b + 1) + _k].append(("conv", B_TILES[_b][1], _k))
        if B_TILES[_b][0] == "u":
            SIDE[4 * (_b + 1) + _k].append(("mean", B_TILES[_b][1], _k))
SEQUENCE = [_e for _slot in SIDE for _e in _slot]

S_USES = ["sumsq1", "hid_k", "hid_v", "kc", "vc", "kc_swap"]
S_USES += [_e for _e in SEQUENCE if _e[0] in ("gate", "cmp_scores", "scores", "cmp_values", "ret_scores", "ret_var", "pool")]
S_USES += ["sumsq2"]
T_USES = ["v_slc", "v_win"]
for _e in SEQUENCE:
    if _e[0] in ("turn", "mix_turn", "ret_turn"):
        T_USES.append(_e)
    if _e[0] == "cmp_turn":
        T_USES += [(*_e, 0), (*_e, 1)]
assert len(S_USES) % 2 == 0 and len(T_USES) % 2 == 0
V_MADE = ["win_k", "win_v", "k0", "k1", "arg_k", "hid_k", "q0", "arg_v", "q1", "hid_v", "q2", "q3", "kc"]
A_MADE = ["hid_k", "hid_v", "gate"]
for _n in range(SLOTS):
    for _e in SIDE[_n]:
        if _e[0] in ("cmp_scores", "scores", "ret_gate", "ret_var") or _e[0] == "ret_values" and _e[2] == QT - 1:
            A_MADE.append(_e)
        if _e[0] == "cmp_scores":
            V_MADE.append(_e)
        if _e[0] == "values" and _e[1] % 16 == 15:
            V_MADE.append(("mix", _e[1] // 16))
        if _e[0] == "mean" and _e[2] == 3:
            V_MADE.append(("u", _e[1]))
    if _n % 4 == 3:
        _b = _n // 4
        if _b and B_TILES[_b - 1][0] in ("rq", "rk"):
            V_MADE.append(B_TILES[_b - 1])
V_MADE.append("branches")
PV = UNITS + RH * QT

def _columns(parts):
    at, out = 0, {}
    for name, n in parts:
        out[name] = at
        at += n
    return out, at


VEC, NVEC = _columns([("norm1", DC), ("norm2", DC), ("b_gate", 4 * DC), ("sc_conv", 3 * BC), ("ret_gn", BC),
                      ("pool_scale", BC), ("ffn_conv", 3 * FC), ("pe", BLOCK), ("w2k", P), ("w2v", P)])
CON, NCON = _columns([("ident", P), ("swap", P), ("ones", P), ("causal", S), ("cmp_mask", QT * NCMP), ("seen", 1),
                      ("eps", 1), ("cos_a", S), ("sin_a", S), ("cos_c", NCMP), ("sin_c", NCMP), ("cos_r", S),
                      ("sin_r", S), ("pool_fix", 16 * 4)])


def build(nc, xT, weights, vec, w1, pool_w, consts, decay, out):
    with ExitStack() as ctx:
        sem = lambda name: ctx.enter_context(nc.semaphore(name))

        KB = 1024
        base = (nc.sbuf_base + 127) // 128 * 128

        def at(name, shape, dt, offset):
            n = 4 * int(np.prod(shape[1:]))
            assert base + offset + n <= nc.sbuf_usable_end, (name, offset)
            return nc.alloc_sbuf_tensor_at(name, shape, dt, offset=base + offset)

        x = at("x", [P, DC, S], F32, 0)
        xg_hi = at("xg_hi", [P, DC, S], F32R, 16 * KB)
        xg_lo = at("xg_lo", [P, DC, S], F32R, 32 * KB)
        w_raw = at("w_raw", [P, RING, CH * P], F32, 48 * KB)
        w_hi = at("w_hi", [P, RING, CH * P], F32R, 60 * KB)
        w_lo = at("w_lo", [P, RING, CH * P], F32R, 72 * KB)
        Y = 84 * KB
        y_hi = [at(f"y_hi{n}", [P, BC, S], F32R, Y + n * 16 * KB) for n in range(4)]
        y_lo = [at(f"y_lo{n}", [P, BC, S], F32R, Y + n * 16 * KB + 8 * KB) for n in range(4)]
        qT = at("qT", [P, 4, S], F32, Y + 48 * KB)
        kT = at("kT", [P, 2, S], F32, Y + 56 * KB)
        v_nat = at("v_nat", [P, 2, QT, P], F32, Y + 60 * KB)
        w1v = at("w1v", [P, BLOCK, P], F32, Y + 32 * KB)
        mixed = at("mixed", [P, S], F32, Y + 32 * KB)
        mix_tmp = at("mix_tmp", [P, S], F32, Y + 34 * KB)
        cmp_pT = at("cmp_pT", [P, 2, S], F32, Y + 36 * KB)
        cmp_p = at("cmp_p", [P, HEADS, NCMP], F32, Y + 40 * KB)
        kc = at("kc", [P, 32], F32, Y + 41 * KB)
        kc_rot = at("kc_rot", [P, 32], F32, Y + 41 * KB + 128)
        vc = at("vc", [32, P], F32, Y + 41 * KB + 256)
        W = Y + 64 * KB
        w1k = at("w1k", [P, BLOCK, P], F32, W)
        rq = at("rq", [P, 2, S], F32, W)
        rk = at("rk", [P, 2, S], F32, W + 4 * KB)
        rv = at("rv", [P, QT, P], F32, W + 8 * KB)
        rv_T = at("rv_T", [P, S], F32, W + 10 * KB)
        rg = at("rg", [P, S], F32, W + 12 * KB)
        rg_t = at("rg_t", [P, S], F32, W + 14 * KB)
        sc = at("sc", [P, 4, S], F32, W + 16 * KB)
        pool_early = at("pool_early", [P, 3, S], F32, Y + 42 * KB)
        rot = at("rot", [P, 2, S], F32, W + 24 * KB)
        pooled = [pool_early[:, 0, :], pool_early[:, 1, :], pool_early[:, 2, :], rot[:, 0, :]]
        dec = at("dec", [P, 2, S], F32, W + 28 * KB)
        k_cmp = at("k_cmp", [P, S], F32, W + 28 * KB)
        v_cmp = at("v_cmp", [P, S], F32, W + 30 * KB)
        mrg_hi = at("mrg_hi", [P, DC, S], F32R, W)
        mrg_lo = at("mrg_lo", [P, DC, S], F32R, W + 16 * KB)
        act_hi = at("act_hi", [P, FC, S], F32R, Y)
        act_lo = at("act_lo", [P, FC, S], F32R, Y + 44 * KB)
        first_sq = at("first_sq", [P, DC, S], F32, Y)
        R = W + 32 * KB
        pr = at("pr", [P, 2, S], F32, R)
        pT = at("pT", [P, 2, S], F32, R + 4 * KB)
        win_k = at("win_k", [P, BLOCK, NCMP], F32, R)
        win_v = at("win_v", [P, BLOCK, NCMP], F32, R + 4 * KB)
        work = at("work", [P, 4, S], F32, R)
        rstd = at("rstd", [P, S], F32, R + 8 * KB)
        ssq = at("ssq", [P, S], F32, R + 10 * KB)
        R2 = R + 12 * KB
        con = at("con", [P, NCON], F32, R2)
        R3 = R2 + (4 * NCON + 31) // 32 * 32
        vc_ = at("vec", [P, NVEC], F32, R3)
        R4 = R3 + (4 * NVEC + 31) // 32 * 32
        gates = at("gates", [P, QT, 3 * HEADS], F32, R4)
        small = at("small", [P, 192], F32, R4 + 4 * QT * 3 * HEADS)
        hid = small[:, 0:NCMP]
        hid_a = small[:, 32:32 + NCMP]
        den = small[:, 64:80]
        nmax = small[:, 80:82]
        c_max = small[:, 82:90]
        c_den = small[:, 90:98]
        scale8 = small[:, 98:106]
        v_sum = small[:, 106:110]
        half_b = small[:, 112:144]
        pad_out = small[:, 144:146]

        def C(name, n, rows=P):
            return con[0:rows, CON[name]:CON[name] + n]

        def V(name, i=0, n=1):
            return vc_[:, VEC[name] + i:VEC[name] + i + n]

        ident, swap, ones = C("ident", P), C("swap", P), C("ones", P)

        bank = lambda name: ctx.enter_context(nc.psum_tensor(name, [P, S], F32))
        acc = [bank(f"acc{i}") for i in range(2)]
        s_bank = [bank(f"s{i}") for i in range(2)]
        t_bank = [bank(f"t{i}") for i in range(2)]
        o_bank = [bank(f"o{i}") for i in range(2)]

        raw_ready = [sem(f"raw_ready{i}") for i in range(RING)]
        hi_ready = sem("hi_ready")
        lo_ready = sem("lo_ready")
        halves = sem("halves")
        acc_free = sem("acc_free")
        s_done, s_free = sem("s_done"), sem("s_free")
        t_done, t_free = sem("t_done"), sem("t_free")
        pv_done, o_free = sem("pv_done"), sem("o_free")
        con_ready = sem("con_ready")
        vec_ready = sem("vec_ready")
        w1_ready = [sem("w1k_ready"), sem("w1v_ready")]
        x_in = [sem(f"x_in{c}") for c in range(DC)]
        pool_w_ready = sem("pool_w_ready")
        dec_ready = [sem("dec_ready0"), sem("dec_ready1")]
        rot_ready = [sem("rot_ready0"), sem("rot_ready1")]
        v_made = sem("v_made")
        a_made = sem("a_made")
        xg_ready = sem("xg_ready")
        ssq_ready = sem("ssq_ready")
        sq_ready = sem("sq_ready")
        root_ready = sem("root_ready")
        ssq_zero = sem("ssq_zero")
        tanh_ready = sem("tanh_ready")
        mrg_ready = sem("mrg_ready")
        conv_ready = sem("conv_ready")
        silu_ready = sem("silu_ready")
        act_ready = sem("act_ready")
        y_ready = sem("y_ready")
        stored = sem("stored")
        rows_done = sem("rows_done")
        passed = sem("passed")
        chain = sem("chain")
        chain_j, chain_f, chain_d = sem("chain_j"), sem("chain_f"), sem("chain_d")

        def s_use(L, name):
            return L * len(S_USES) + S_USES.index(name) + 1

        def t_use(L, name):
            return L * len(T_USES) + T_USES.index(name) + 1

        def v_count(L, name):
            return L * len(V_MADE) + V_MADE.index(name) + 1

        def a_count(L, name):
            return L * len(A_MADE) + A_MADE.index(name) + 1

        def s_of(name):
            return s_bank[S_USES.index(name) % 2]

        def t_of(name):
            return t_bank[T_USES.index(name) % 2]

        ROT = {n: i for i, n in enumerate(["k0", "k1", "q0", "q1", "q2", "q3"])}
        for h in range(RH):
            ROT[("rq", h)], ROT[("rk", h)] = 6 + 2 * h, 7 + 2 * h
        ROT_DMA = 16 * (3 * 4 + RH * 2)

        def rot_value(L, name):
            i = ROT[name] // 2
            return L * ROT_DMA + 16 * (4 * (i + 1) if i < 3 else 12 + 2 * (i - 2))

        A_AT = {"k0": 2, "k1": 3, "q0": 6, "q1": 7, "q2": 8, "q3": 9}

        def alone(engine):
            engine.sem_inc(passed, 1)

        def unit(u):
            return u // 16, u % 16 // HEADS, u % HEADS // 2 + 4 * (u % 2)

        block = ctx.enter_context(nc.Block())

        @block.sync
        def _(sp):
            def load_group(g, slot):
                sp.dma_start(w_raw[:, slot, :],
                             weights[bass.ds(g, 1), :, :].rearrange("a p n -> (a p) n")).then_inc(raw_ready[slot], 16)

            def load_groups(L, first, last):
                with sp.Fori(0, (last - first) // RING) as t:
                    for k in range(RING):
                        g = L * GROUPS + t * RING + (first + k)
                        sp.wait_ge(lo_ready, 1 + g - (RING - 1))
                        load_group(g + 0, (first + k) % RING)

            sp.dma_start(vc_[:, :], vec[0, :, :]).then_inc(vec_ready, 16)
            sp.dma_start(x[:, 0, :], xT[:, 0, :]).then_inc(x_in[0], 16)
            load_group(0, 0)
            for c in range(1, DC):
                sp.dma_start(x[:, c, :], xT[:, c, :]).then_inc(x_in[c], 16)
            load_group(1, 1)
            sp.dma_start(con[:, :], consts).then_inc(con_ready, 16)
            load_group(2, 2)
            with sp.Fori(0, LAYERS) as L:
                sp.wait_ge(halves, 1 + L * (2 * GROUPS))
                sp.dma_start(w1k[:, :, :], w1[bass.ds(L * 2, 1), :, :, :].rearrange("a p l n -> (a p) l n")).then_inc(w1_ready[0], 16)
                sp.dma_start(w1v[:, :, :], w1[bass.ds(L * 2 + 1, 1), :, :, :].rearrange("a p l n -> (a p) l n")).then_inc(w1_ready[1], 16)
                load_groups(L, RING, D0 + RING)
                sp.wait_ge(act_ready, 1 + L * FC + FC)
                sp.dma_start(vc_[:, :], vec[bass.ds(L + 1, 1), :, :].rearrange("a p n -> (a p) n")).then_inc(vec_ready, 16)
                load_groups(L, D0 + RING, GROUPS + RING)
            for c in range(DC):
                sp.wait_ge(y_ready, c + 1)
                sp.dma_start(out[:, c, :], x[:, c, :]).then_inc(stored, 16)
            sp.wait_ge(stored, 16 * DC)

        @block.gpsimd
        def _(pool):
            pool.sem_inc(lo_ready, 1)
            with pool.Fori(0, LAYERS * GROUPS // RING) as t:
                for k in range(RING):
                    pool.wait_ge(hi_ready, t * RING + (k + 1))
                    nc.gpsimd.tensor_tensor(w_lo[:, k, :], w_raw[:, k, :], w_hi[:, k, :].bitcast(F32),
                                            ALU.subtract).then_inc(lo_ready, 1)

        @block.scalar
        def _(act):
            def ahead(L, g, loop=None, per=0):
                at_g = L * (2 * GROUPS) + 2 * g
                turns = L * (16 * GROUPS // RING) + 16 * ((g + 2) // RING + 1)
                if loop is not None:
                    at_g = at_g + loop * (2 * per)
                    turns = turns + loop * (16 * per // RING)
                slot = (g + 2) % RING
                act.wait_ge(halves, 1 + at_g)
                act.wait_ge(raw_ready[slot], turns)
                nc.scalar.activation(w_hi[:, slot, :], w_raw[:, slot, :], ACT.Copy).then_inc(hi_ready, 1)

            def root(use, L):
                act.wait_ge(s_done, s_use(L, use))
                act.wait_ge(con_ready, 16)
                nc.scalar.activation(rstd[:, :], s_of(use)[:, :], ACT.Sqrt, bias=C("eps", 1),
                                     scale=1.0 / D).then_inc(root_ready, 1)

            def rotate_partners(L, name):
                i = ROT[name]
                dst = rot[:, i % 2, :]
                if isinstance(name, str):
                    act.wait_ge(acc_free, 1 + L * TILES + (A_AT[name] + 2))
                    if i >= 2:
                        before = [n for n, k in ROT.items() if k == i - 2][0]
                        act.wait_ge(v_made, v_count(L, before))
                    src = kT[:, int(name[1]), :] if name[0] == "k" else qT[:, int(name[1]), :]
                    for g in range(KV_GROUPS):
                        o = 64 * g
                        act.dma_start(dst[o:o + 8, :], src[o + 8:o + 16, :]).then_inc(rot_ready[i % 2], 16)
                        act.dma_start(dst[o + 8:o + 16, :], src[o:o + 8, :]).then_inc(rot_ready[i % 2], 16)
                else:
                    act.wait_ge(acc_free, 1 + L * TILES + (A_GROUPS + B_TILES.index(name) + 2))
                    before = [n for n, k in ROT.items() if k == i - 2][0]
                    act.wait_ge(v_made, v_count(L, before))
                    src = (rq if name[0] == "rq" else rk)[:, name[1] % 2, :]
                    act.dma_start(dst[0:64, :], src[64:128, :]).then_inc(rot_ready[i % 2], 16)
                    act.dma_start(dst[64:128, :], src[0:64, :]).then_inc(rot_ready[i % 2], 16)

            for c in range(DC):
                if c in (0, 4):
                    act.wait_ge(raw_ready[c // 4], 16)
                    nc.scalar.activation(w_hi[:, c // 4, :], w_raw[:, c // 4, :], ACT.Copy).then_inc(hi_ready, 1)
                act.wait_ge(x_in[c], 16)
                nc.scalar.activation(first_sq[:, c, :], x[:, c, :], ACT.Square).then_inc(sq_ready, 1)

            with act.Fori(0, LAYERS) as L:
                for g in range(A_GROUPS):
                    ahead(L, g)
                    if g == 0:
                        root("sumsq1", L)
                    for name in ("k0", "k1", "q0", "q1", "q2", "q3"):
                        if A_AT[name] == g - 1:
                            rotate_partners(L, name)
                    if g in (5, 8):
                        kind = "k" if g == 5 else "v"
                        act.wait_ge(v_made, v_count(L, f"arg_{kind}"))
                        nc.scalar.activation(hid_a, hid_a, ACT.Tanh, scale=0.7978845608028654).then_inc(a_made, 1)
                    if g == 11:
                        act.wait_ge(acc_free, 1 + L * TILES + 12)
                        nc.scalar.activation(sc[:, 2, :], sc[:, 2, :], ACT.Tanh, scale=0.5).then_inc(a_made, 1)

                for b in range(B_GROUPS):
                    ahead(L, A_GROUPS + b)
                    if 0 < b and B_TILES[b - 1][0] in ("rq", "rk"):
                        rotate_partners(L, B_TILES[b - 1])
                    for h in range(RH):
                        if b == 14 + 4 * h:
                            if h >= 2:
                                act.wait_ge(s_free, 1 + s_use(L, ("ret_scores", h - 2, QT - 1)) + 1)
                            act.dma_start(dec[:, h % 2, :], decay[h, :, :]).then_inc(dec_ready[h % 2], 16)
                    if b == 15:
                        act.wait_ge(acc_free, 1 + L * TILES + (A_GROUPS + 15))
                        act.dma_start(sc[:, 3, :].rearrange("p (g n) -> p g n", g=4),
                                      pool_w[bass.ds(L, 1), :, :, :].rearrange("a p g n -> (a p) g n")).then_inc(pool_w_ready, 16)
                    for n in range(4 * b, 4 * b + 4):
                        for e in SIDE[n]:
                            if e[0] == "cmp_scores":
                                act.wait_ge(v_made, v_count(L, e))
                                nc.scalar.activation(cmp_p[:, :, :], cmp_p[:, :, :], ACT.Exp,
                                                     scale=DH ** -0.5).then_inc(a_made, 1)
                            elif e[0] == "scores":
                                u = e[1]
                                w = (unit(u)[0] + 1) * P
                                _, br, h = unit(u)
                                act.wait_ge(s_free, 1 + s_use(L, e) + 1)
                                nc.scalar.activation(pr[:, u % 2, 0:w], pr[:, u % 2, 0:w], ACT.Exp,
                                                     bias=nmax[:, u % 2:u % 2 + 1], scale=-1.0,
                                                     accum_out=den[:, 8 * br + h:8 * br + h + 1]).then_inc(a_made, 1)
                            elif e[0] == "ret_gate":
                                act.wait_ge(acc_free, 1 + L * TILES + (A_GROUPS + B_TILES.index(("rg", e[1])) + 2))
                                nc.scalar.activation(rg_t[:, :], rg[:, :], ACT.Tanh, scale=0.5).then_inc(a_made, 1)
                            elif e[0] == "ret_values" and e[2] == QT - 1:
                                act.wait_ge(o_free, 1 + L * (2 * QT + RH) + (2 * QT + e[1] + 2))
                                nc.scalar.activation(pT[:, 1, :], pT[:, 0, :], ACT.Square).then_inc(a_made, 1)
                            elif e[0] == "ret_var":
                                act.wait_ge(s_done, s_use(L, e))
                                act.wait_ge(con_ready, 16)
                                nc.scalar.activation(pT[:, 1, :], s_of(e)[:, :], ACT.Sqrt, bias=C("eps", 1),
                                                     scale=1.0 / RD).then_inc(a_made, 1)

                with act.Fori(0, DC) as j:
                    for k in range(J_GROUPS):
                        ahead(L, J0 + k, j, J_GROUPS)
                        if 1 <= k <= 4:
                            n = k - 1
                            act.wait_ge(acc_free, 1 + L * TILES + j * 8 + (TJ0 + n + 2))
                            act.wait_ge(con_ready, 16)
                            nc.scalar.activation(work[:, n, :], work[:, n, :], ACT.Tanh, scale=0.5,
                                                 bias=half_b[:, bass.ds(j + n * DC, 1)]).then_inc(tanh_ready, 1)

                for j in range(DC):
                    ahead(L, O0 + j)
                    if j:
                        act.wait_ge(acc_free, 1 + L * TILES + (TO0 + j + 1))
                        nc.scalar.activation(work[:, 2 + (j - 1) % 2, :], x[:, j - 1, :], ACT.Square).then_inc(sq_ready, 1)

                def up(i, g, loop=None):
                    for k in range(2):
                        if loop is None:
                            ahead(L, g + k)
                        else:
                            ahead(L, g + k, loop, 2 * 3)
                        if i is None and k == 0:
                            act.wait_ge(acc_free, 1 + L * TILES + (TO0 + DC + 1))
                            nc.scalar.activation(work[:, 2 + (DC - 1) % 2, :], x[:, DC - 1, :], ACT.Square).then_inc(sq_ready, 1)
                        if i is None and k == 0:
                            root("sumsq2", L)
                        if k == 1:
                            act.wait_ge(conv_ready, L * FC + (1 if i is None else i + 1))
                            nc.scalar.activation(work[:, 2, :], work[:, 1, :], ACT.Tanh, scale=0.5).then_inc(silu_ready, 1)

                up(None, U0)
                with act.Fori(0, (FC - 1) // 3) as t:
                    for k in range(3):
                        up(t * 3 + (k + 1), U0 + 2 + 2 * k, t)

                with act.Fori(0, DC // 2) as t:
                    for k in range(2):
                        for m in range(DG):
                            ahead(L, D0 + DG * k + m, t, 2 * DG)
                        act.wait_ge(acc_free, 1 + L * TILES + t * 2 + (TD0 + k + 2))
                        act.wait_ge(con_ready, 16)
                        nc.scalar.activation(work[:, 2 + k, :], x[:, bass.ds(t * 2 + k, 1), :], ACT.Square).then_inc(sq_ready, 1)

            act.wait_ge(s_done, LAYERS * len(S_USES) + 1)
            nc.scalar.activation(rstd[:, :], s_bank[0][:, :], ACT.Sqrt, bias=C("eps", 1),
                                 scale=1.0 / D).then_inc(root_ready, 1)

        @block.vector
        def _(dve):
            ve = nc.vector
            made = {"s": 0, "t": 0, "v": 0}

            class Chain:

                def __init__(self, s):
                    self.s, self.base, self.n = s, 0, 0

                def __call__(self, ins):
                    self.n += 1
                    ins.then_inc(self.s, 1)
                    dve.wait_ge(self.s, self.base + self.n)

                def turn(self, base, n):
                    self.base, self.n, self.per = base, 0, n

                def end(self):
                    assert self.n == self.per, (self.s, self.n)

            then = Chain(chain)

            def split_x(c, gain, x_c, hi, lo):
                then_ = current[0]
                then_(ve.tensor_scalar(hi, x_c, gain, None, ALU.mult))
                ve.scalar_tensor_tensor(out=lo, in0=x_c, scalar=gain, in1=hi.bitcast(F32),
                                        op0=ALU.mult, op1=ALU.subtract).then_inc(xg_ready, 1)

            current = [then]
            for s in (acc_free, s_free, t_free, o_free, pv_done):
                dve.sem_inc(s, 2)
            for s in (mrg_ready, act_ready):
                dve.sem_inc(s, 1)
            then(ve.memset(small[:, :], 0.0))
            dve.wait_ge(vec_ready, 16)
            for c in range(DC):
                dve.wait_ge(x_in[c], 16)
                split_x(c, V("norm1", c), x[:, c, :], xg_hi[:, c, :], xg_lo[:, c, :])
            for c in range(DC):
                dve.wait_ge(sq_ready, c + 1)
                if c == 0:
                    ve.tensor_copy(ssq[:, :], first_sq[:, 0, :]).then_inc(ssq_ready, 1)
                else:
                    dve.wait_ge(ssq_ready, c)
                    ve.tensor_tensor(ssq[:, :], ssq[:, :], first_sq[:, c, :], ALU.add).then_inc(ssq_ready, 1)
            CHAIN0 = then.n
            SSQ0 = DC

            with dve.Fori(0, LAYERS) as L:
                then.turn(CHAIN0 + L * CHAIN_LAYER, CHAIN_LAYER)
                current[0] = then

                def take(T, out, in1=None, op=ALU.mult, count=None):
                    dve.wait_ge(halves, 1 + L * (2 * GROUPS) + 2 * (T + 1))
                    ve.tensor_tensor(out, acc[T % 2][0:out.shape[0], :], rstd[0:out.shape[0], :], op).then_inc(acc_free, 1)
                    dve.wait_ge(acc_free, 1 + L * TILES + (T + 2))

                def s_wait(name):
                    dve.wait_ge(s_done, s_use(L, name))

                def s_end(ins, name, wait=False):
                    made["s"] += 1
                    assert S_USES.index(name) + 1 == made["s"], name
                    ins.then_inc(s_free, 1)
                    if wait:
                        dve.wait_ge(s_free, 1 + s_use(L, name) + 1)

                def t_wait(name):
                    dve.wait_ge(t_done, t_use(L, name))

                def t_end(ins, name):
                    made["t"] += 1
                    assert T_USES.index(name) + 1 == made["t"], name
                    ins.then_inc(t_free, 1)

                def v_end(ins, name, wait=False):
                    made["v"] += 1
                    assert V_MADE.index(name) + 1 == made["v"], name
                    ins.then_inc(v_made, 1)
                    if wait:
                        dve.wait_ge(v_made, v_count(L, name))

                def inverse_root(use, n):
                    dve.wait_ge(root_ready, 2 * L + (n + 1))
                    ins = ve.reciprocal(rstd[:, :], rstd[:, :])
                    s_end(ins, use, wait=True)

                def rotate(name, z, cos, sin):
                    i = ROT[name]
                    dve.wait_ge(rot_ready[i % 2], rot_value(L, name))
                    r = rot[:, i % 2, :]
                    ve.tensor_tensor(r, r, C(sin, S), ALU.mult).then_inc(chain, 1)
                    then.n += 1
                    then(ve.tensor_tensor(z, z, C(cos, S), ALU.mult))
                    v_end(ve.tensor_tensor(z, z, r, ALU.add), name)

                def windows(src, dst, name):
                    view = src.rearrange("p (m r) -> p r m", r=STRIDE)
                    for a in range(2):
                        pe_ = V("pe", a * STRIDE, STRIDE).unsqueeze(2).to_broadcast([P, STRIDE, NCMP])
                        ins = ve.tensor_tensor(dst[:, a * STRIDE:(a + 1) * STRIDE, :], view[:, :, a:a + NCMP], pe_, ALU.add)
                        if a == 0:
                            ins.then_inc(chain, 1)
                            then.n += 1
                    v_end(ins, name)

                def gelu_arg(kind):
                    s_wait(f"hid_{kind}")
                    s_end(ve.tensor_copy(hid, s_of(f"hid_{kind}")[:, 0:NCMP]), f"hid_{kind}", wait=True)
                    then(ve.tensor_tensor(hid_a, hid, hid, ALU.mult))
                    then(ve.tensor_scalar(hid_a, hid_a, 0.044715, 1.0, ALU.mult, ALU.add))
                    v_end(ve.tensor_tensor(hid_a, hid_a, hid, ALU.mult), f"arg_{kind}")

                def gelu(kind):
                    dve.wait_ge(a_made, a_count(L, f"hid_{kind}"))
                    v_end(ve.scalar_tensor_tensor(out=hid, in0=hid_a, scalar=1.0, in1=hid,
                                                  op0=ALU.add, op1=ALU.mult), f"hid_{kind}")

                made.update(s=0, t=0, v=0)
                dve.wait_ge(con_ready, 16)
                dve.wait_ge(vec_ready, L * 16 + 16)
                then(ve.tensor_scalar(half_b, V("b_gate", 0, 4 * DC), 0.5, None, ALU.mult))
                then(ve.memset(rot[:, :, :], 0.0))
                inverse_root("sumsq1", 0)
                take(0, k_cmp[:, :])
                take(1, v_cmp[:, :])
                windows(k_cmp[:, :], win_k, "win_k")
                take(2, kT[:, 0, :])
                windows(v_cmp[:, :], win_v, "win_v")
                take(3, kT[:, 1, :])
                rotate("k0", kT[:, 0, :], "cos_a", "sin_a")
                take(4, sc[:, 0, :])
                rotate("k1", kT[:, 1, :], "cos_a", "sin_a")
                gelu_arg("k")
                take(5, sc[:, 1, :])
                gelu("k")
                t_wait("v_slc")
                t_end(ve.tensor_copy(v_nat[:, 0, :, :], t_of("v_slc")[:, :].rearrange("p (k n) -> p k n", k=QT)), "v_slc")
                take(6, qT[:, 0, :])
                take(7, qT[:, 1, :])
                t_wait("v_win")
                t_end(ve.tensor_copy(v_nat[:, 1, :, :], t_of("v_win")[:, :].rearrange("p (k n) -> p k n", k=QT)), "v_win")
                rotate("q0", qT[:, 0, :], "cos_a", "sin_a")
                s_wait("kc")
                gelu_arg("v")
                s_end(ve.tensor_scalar(kc[:, 0:NCMP], s_of("kc")[:, 0:NCMP], 0.5, None, ALU.mult), "kc")
                take(8, qT[:, 2, :])
                rotate("q1", qT[:, 1, :], "cos_a", "sin_a")
                gelu("v")
                take(9, qT[:, 3, :])
                rotate("q2", qT[:, 2, :], "cos_a", "sin_a")
                s_wait("vc")
                s_end(ve.tensor_scalar(vc[0:NCMP, :], s_of("vc")[0:NCMP, 0:P], 0.5, None, ALU.mult), "vc")
                s_wait("kc_swap")
                s_end(ve.tensor_tensor(kc_rot[:, 0:NCMP], s_of("kc_swap")[:, 0:NCMP], C("sin_c", NCMP), ALU.mult), "kc_swap", wait=True)
                then(ve.tensor_tensor(kc[:, 0:NCMP], kc[:, 0:NCMP], C("cos_c", NCMP), ALU.mult))
                take(10, sc[:, 2, :])
                rotate("q3", qT[:, 3, :], "cos_a", "sin_a")
                v_end(ve.tensor_tensor(kc[:, 0:NCMP], kc[:, 0:NCMP], kc_rot[:, 0:NCMP], ALU.add), "kc")
                dve.wait_ge(halves, 1 + L * (2 * GROUPS) + 24)
                ve.tensor_copy(pad_out, acc[1][:, 0:2]).then_inc(acc_free, 1)

                def gate(e):
                    s_wait(e)
                    s_end(ve.tensor_scalar(gates[:, :, :], s_of(e)[:, :].rearrange("p (k n) -> p k n", k=QT)[:, :, 0:3 * HEADS],
                                           1.0, 0.5, ALU.add, ALU.mult), e, wait=True)

                def gate_over_sum(qi, branch, sums):
                    then(ve.reciprocal(scale8, sums))
                    g3 = gates[:, qi, :].rearrange("p (h b) -> p b h", b=3)[:, branch, :]
                    then(ve.tensor_tensor(scale8, scale8, g3, ALU.mult))

                def heads(ap):
                    return ap.rearrange("p (h d) -> p h d", h=HEADS)

                def by_head():
                    return scale8.unsqueeze(2).to_broadcast([P, HEADS, DH])

                def cmp_scores(e):
                    qi = e[1]
                    s_wait(e)
                    src = s_of(e)[:, 0:HEADS * 32].rearrange("p (h n) -> p h n", h=HEADS)[:, :, 0:NCMP]
                    m = C("cmp_mask", QT * NCMP).rearrange("p (q n) -> p q n", q=QT)[:, qi, :]
                    s_end(ve.tensor_tensor(cmp_p[:, :, :], src, m.unsqueeze(1).to_broadcast([P, HEADS, NCMP]), ALU.add), e, wait=True)
                    then(ve.tensor_reduce(c_max, cmp_p[:, :, :], AX.X, ALU.max))
                    v_end(ve.tensor_tensor(cmp_p[:, :, :], cmp_p[:, :, :], c_max.unsqueeze(2).to_broadcast([P, HEADS, NCMP]),
                                           ALU.subtract), e)

                def scores(e):
                    u = e[1]
                    w = (unit(u)[0] + 1) * P
                    s_wait(e)
                    alone(dve)
                    s_end(ve.tensor_tensor_reduce(pr[:, u % 2, 0:w], s_of(e)[:, 0:w], C("causal", S)[:, S - w:S],
                                                  -(DH ** -0.5), 3e38, ALU.add, ALU.min, nmax[:, u % 2:u % 2 + 1]), e)

                def turn(e):
                    u = e[1]
                    w = (unit(u)[0] + 1) * P
                    t_wait(e)
                    dve.wait_ge(pv_done, 1 + L * PV + u)
                    t_end(ve.tensor_copy(pT[:, u % 2, 0:w], t_of(e)[:, 0:w]), e)

                def values(e):
                    u = e[1]
                    if u % 8 != 7:
                        return
                    qi, br, _ = unit(u)
                    dve.wait_ge(a_made, a_count(L, ("scores", u)))
                    gate_over_sum(qi, 1 + br, den[:, 8 * br:8 * br + 8])
                    dve.wait_ge(pv_done, 1 + L * PV + (u + 2))
                    ve.tensor_tensor(heads(mix_tmp[:, :]), heads(o_bank[br][:, :]), by_head(), ALU.mult).then_inc(o_free, 1)
                    dve.wait_ge(o_free, 1 + L * (2 * QT + RH) + (2 * qi + br + 2))
                    ins = ve.tensor_tensor(mixed[:, :], mixed[:, :], mix_tmp[:, :], ALU.add)
                    if br == 0:
                        then(ins)
                    else:
                        v_end(ins, ("mix", qi))

                def cmp_turn(e):
                    for half in range(2):
                        t_wait((*e, half))
                        t_end(ve.tensor_copy(cmp_pT[0:NCMP, half, :], t_of((*e, half))[0:NCMP, :]), (*e, half))

                def cmp_values(e):
                    qi = e[1]
                    then(ve.tensor_reduce(c_den, cmp_p[:, :, :], AX.X, ALU.add))
                    gate_over_sum(qi, 0, c_den)
                    if qi == 0:
                        then(ve.tensor_scalar(scale8, scale8, C("seen", 1), None, ALU.mult))
                    s_wait(e)
                    s_end(ve.tensor_tensor(heads(mixed[:, :]), heads(s_of(e)[:, :]), by_head(), ALU.mult), e, wait=True)

                def mix_turn(e):
                    qi = e[1]
                    t_wait(e)
                    src = t_of(e)[:, :].rearrange("p (j n) -> p j n", j=BC)
                    hi, lo = (y[1][:, :, qi * P:(qi + 1) * P] for y in (y_hi, y_lo))
                    then(ve.tensor_copy(hi, src))
                    t_end(ve.tensor_tensor(lo, src, hi.bitcast(F32), ALU.subtract), e)

                def ret_scores(e):
                    h, m = e[1], e[2]
                    w = S - m * P
                    s_wait(e)
                    if m == 0:
                        dve.wait_ge(dec_ready[h % 2], L * 32 + 16 * (h // 2 + 1))
                    r = QT * h + m
                    dve.wait_ge(pv_done, 1 + L * PV + (UNITS + r))
                    s_end(ve.tensor_tensor(pr[:, m % 2, 0:w], s_of(e)[:, 0:w], dec[:, h % 2, 0:w], ALU.mult), e)

                def ret_values(e):
                    h, m = e[1], e[2]
                    if m < QT - 1:
                        return
                    dve.wait_ge(pv_done, 1 + L * PV + (UNITS + QT * h + QT + 1))
                    ve.tensor_copy(pT[:, 0, :], o_bank[h % 2][:, :]).then_inc(o_free, 1)
                    dve.wait_ge(o_free, 1 + L * (2 * QT + RH) + (2 * QT + h + 2))

                def ret_turn(e):
                    t_wait(e)
                    src = t_of(e)[:, :].rearrange("p (k n) -> p k n", k=QT)
                    then(ve.tensor_reduce(v_sum, src, AX.X, ALU.add))
                    t_end(ve.scalar_tensor_tensor(out=rv[:, :, :], in0=v_sum.unsqueeze(2).to_broadcast([P, QT, RD]),
                                                  scalar=-1.0 / RD, in1=src, op0=ALU.mult, op1=ALU.add), e)

                def ret_gate(e):
                    dve.wait_ge(a_made, a_count(L, e))
                    then(ve.scalar_tensor_tensor(out=rg[:, :], in0=rg_t[:, :], scalar=1.0, in1=rg[:, :],
                                                 op0=ALU.add, op1=ALU.mult))

                def ret_var(e):
                    dve.wait_ge(a_made, a_count(L, e))
                    s_end(ve.reciprocal(pT[:, 1, :], pT[:, 1, :]), e, wait=True)

                def split_y(n, j, src):
                    hi, lo = y_hi[n][:, j, :], y_lo[n][:, j, :]
                    then(ve.tensor_copy(hi, src))
                    then(ve.tensor_tensor(lo, src, hi.bitcast(F32), ALU.subtract))

                def ret_end(e):
                    h = e[1]
                    o = pT[:, 0, :]
                    then(ve.scalar_tensor_tensor(out=o, in0=o, scalar=V("ret_gn", h), in1=pT[:, 1, :],
                                                 op0=ALU.mult, op1=ALU.mult))
                    then(ve.scalar_tensor_tensor(out=o, in0=o, scalar=0.5, in1=rg[:, :], op0=ALU.mult, op1=ALU.mult))
                    split_y(2, h, o)

                def pool(e):
                    g = e[1]
                    s_wait(e)
                    sc_ = V("pool_scale", g)
                    hi, lo = y_hi[3][:, g, :], y_lo[3][:, g, :]
                    then(ve.tensor_scalar(hi, s_of(e)[:, :], sc_, None, ALU.mult))
                    s_end(ve.scalar_tensor_tensor(out=lo, in0=s_of(e)[:, :], scalar=sc_, in1=hi.bitcast(F32),
                                                  op0=ALU.mult, op1=ALU.subtract), e)

                def conv(e):
                    j, part = e[1], e[2]
                    t, y, b = sc[:, 1, :], sc[:, 2, :], sc[:, 3, :]
                    tap = lambda k: V("sc_conv", 3 * j + k)
                    hi, lo = y_hi[0][:, j, :], y_lo[0][:, j, :]
                    if part == 0:
                        then(ve.tensor_scalar(y, t, tap(2), None, ALU.mult))
                        then(ve.scalar_tensor_tensor(out=y[:, 1:S], in0=t[:, 0:S - 1], scalar=tap(1), in1=y[:, 1:S], op0=ALU.mult, op1=ALU.add))
                    elif part == 1:
                        then(ve.scalar_tensor_tensor(out=y[:, 2:S], in0=t[:, 0:S - 2], scalar=tap(0), in1=y[:, 2:S], op0=ALU.mult, op1=ALU.add))
                        then(ve.tensor_tensor(y, y, b, ALU.mult))
                    elif part == 2:
                        then(ve.tensor_copy(hi, y))
                    else:
                        then(ve.tensor_tensor(lo, y, hi.bitcast(F32), ALU.subtract))

                def mean(e):
                    g, part = e[1], e[2]
                    u, n = sc[:, 0, :], POOLS[g]
                    buf = lambda k: u if k == 0 else sc[:, 1 + k % 2, :]
                    if part <= g:
                        src, dst, k = buf(part), buf(part + 1), 1 << part
                        then(ve.tensor_copy(dst[:, 0:k], src[:, 0:k]))
                        then(ve.tensor_tensor(dst[:, k:S], src[:, k:S], src[:, 0:S - k], ALU.add))
                    if part == 3:
                        src = buf(g + 1)
                        fix = C("pool_fix", 64)[:, 16 * g:16 * g + n - 1]
                        then(ve.tensor_tensor(src[:, 0:n - 1], src[:, 0:n - 1], fix, ALU.mult))
                        v_end(ve.scalar_tensor_tensor(out=pooled[g], in0=src, scalar=1.0 / n, in1=u, op0=ALU.mult, op1=ALU.subtract),
                              ("u", g), wait=True)

                steps = {"gate": gate, "cmp_scores": cmp_scores, "scores": scores, "turn": turn, "values": values,
                         "cmp_turn": cmp_turn, "cmp_values": cmp_values, "mix_turn": mix_turn, "ret_scores": ret_scores,
                         "ret_values": ret_values, "ret_turn": ret_turn, "ret_gate": ret_gate, "ret_var": ret_var,
                         "ret_end": ret_end, "pool": pool, "conv": conv, "mean": mean}

                for b in range(B_GROUPS):
                    for n in range(4 * b, 4 * b + 4):
                        for e in SIDE[n]:
                            steps[e[0]](e)
                    kind, i = B_TILES[b]
                    T = A_GROUPS + b
                    take(T, {"rq": rq[:, i % 2, :], "rk": rk[:, i % 2, :], "rv": rv_T[:, :], "rg": rg[:, :], "c": sc[:, 0, :],
                             "h": sc[:, 1, :], "b": sc[:, 3, :], "u": sc[:, 0, :]}[kind])
                    if b and B_TILES[b - 1][0] in ("rq", "rk"):
                        k2, h2 = B_TILES[b - 1]
                        rotate((k2, h2), (rq if k2 == "rq" else rk)[:, h2 % 2, :], "cos_r", "sin_r")
                    if kind == "h":
                        then(ve.tensor_tensor(sc[:, 1, :], sc[:, 1, :], sc[:, 0, :], ALU.mult))
                for k in range(4):
                    conv(("conv", B_TILES[-1][1], k))
                v_end(ve.memset(ssq[:, :], 0.0), "branches")

                with dve.Fori(0, DC) as j:
                    cj = Chain(chain_j)
                    cj.turn(L * (DC * CHAIN_J) + j * CHAIN_J, CHAIN_J)
                    dve.wait_ge(mrg_ready, 1 + L * DC + j)
                    for n in range(4):
                        dve.wait_ge(halves, 1 + L * (2 * GROUPS) + j * (2 * J_GROUPS) + (2 * J0 + 2 * (n + 1)))
                        ve.tensor_tensor(work[:, n, :], acc[n % 2][:, :], rstd[:, :], ALU.mult).then_inc(acc_free, 1)
                        dve.wait_ge(acc_free, 1 + L * TILES + j * 8 + (TJ0 + n + 2))
                    for n in range(4):
                        dve.wait_ge(tanh_ready, L * (4 * DC) + j * 4 + (n + 1))
                        dve.wait_ge(halves, 1 + L * (2 * GROUPS) + j * (2 * J_GROUPS) + (2 * J0 + 8 + (n + 1)))
                        ve.scalar_tensor_tensor(out=work[:, n, :], in0=work[:, n, :], scalar=1.0, in1=acc[n % 2][:, :],
                                                op0=ALU.add, op1=ALU.mult).then_inc(acc_free, 1)
                        dve.wait_ge(acc_free, 1 + L * TILES + j * 8 + (TJ0 + 4 + n + 2))
                        if n:
                            cj(ve.tensor_tensor(work[:, 0, :], work[:, 0, :], work[:, n, :], ALU.add))
                    hi, lo = mrg_hi[:, bass.ds(j, 1), :], mrg_lo[:, bass.ds(j, 1), :]
                    src = work[:, 0:1, :]
                    alone(dve)
                    cj(ve.tensor_copy(hi, src))
                    ve.tensor_tensor(lo, src, hi.bitcast(F32), ALU.subtract).then_inc(mrg_ready, 1)
                    cj.end()

                def add_square(buf, value, c):
                    dve.wait_ge(sq_ready, value)
                    dve.wait_ge(ssq_ready, value - 1)
                    ve.tensor_tensor(ssq[:, :], ssq[:, :], work[:, buf, :], ALU.add).then_inc(ssq_ready, 1)

                dve.wait_ge(v_made, v_count(L, "branches"))
                for j in range(DC):
                    T = TO0 + j
                    dve.wait_ge(halves, 1 + L * (2 * GROUPS) + 2 * (O0 + j + 1))
                    ve.scalar_tensor_tensor(out=x[:, j, :], in0=acc[T % 2][:, :], scalar=0.5, in1=x[:, j, :],
                                            op0=ALU.mult, op1=ALU.add).then_inc(acc_free, 1)
                    dve.wait_ge(acc_free, 1 + L * TILES + (T + 2))
                    split_x(j, V("norm2", j), x[:, j, :], xg_hi[:, j, :], xg_lo[:, j, :])
                    if j:
                        add_square(2 + (j - 1) % 2, L * 16 + (SSQ0 + j), j)
                add_square(2 + (DC - 1) % 2, L * 16 + (SSQ0 + DC), DC)

                def up(i, T_gate, cf, halves_gate, acc_gate):
                    u, c, t, v = (work[:, k, :] for k in range(4))
                    tap = lambda k: (V("ffn_conv", 3 * i + k) if isinstance(i, int)
                                     else vc_[:, bass.ds(i * 3 + (VEC["ffn_conv"] + k), 1)])
                    dve.wait_ge(act_ready, 1 + L * FC + i)
                    dve.wait_ge(halves, 1 + halves_gate)
                    ve.tensor_tensor(u, acc[0][:, :], rstd[:, :], ALU.mult).then_inc(acc_free, 1)
                    dve.wait_ge(acc_free, 1 + acc_gate)
                    cf(ve.tensor_scalar(c, u, tap(2), None, ALU.mult))
                    cf(ve.scalar_tensor_tensor(out=c[:, 1:S], in0=u[:, 0:S - 1], scalar=tap(1), in1=c[:, 1:S], op0=ALU.mult, op1=ALU.add))
                    ve.scalar_tensor_tensor(out=c[:, 2:S], in0=u[:, 0:S - 2], scalar=tap(0), in1=c[:, 2:S],
                                            op0=ALU.mult, op1=ALU.add).then_inc(conv_ready, 1)
                    dve.wait_ge(silu_ready, L * FC + (i + 1))
                    cf(ve.scalar_tensor_tensor(out=t, in0=t, scalar=1.0, in1=c, op0=ALU.add, op1=ALU.mult))
                    dve.wait_ge(halves, 1 + halves_gate + 2)
                    ve.tensor_tensor(v, acc[1][:, :], rstd[:, :], ALU.mult).then_inc(acc_free, 1)
                    dve.wait_ge(acc_free, 1 + acc_gate + 1)
                    cf(ve.tensor_tensor(t, t, v, ALU.mult))
                    if isinstance(i, int):
                        hi, lo, t3 = act_hi[:, i, :], act_lo[:, i, :], t
                    else:
                        hi, lo, t3 = act_hi[:, bass.ds(i, 1), :], act_lo[:, bass.ds(i, 1), :], work[:, 2:3, :]
                    alone(dve)
                    cf(ve.tensor_copy(hi, t3))
                    ve.tensor_tensor(lo, t3, hi.bitcast(F32), ALU.subtract).then_inc(act_ready, 1)

                inverse_root("sumsq2", 1)
                assert made == {"s": len(S_USES), "t": len(T_USES), "v": len(V_MADE)}
                up(0, TU0, then, L * (2 * GROUPS) + 2 * (U0 + 1), L * TILES + (TU0 + 2))
                then.end()
                alone(dve)
                with dve.Fori(0, (FC - 1) // 3) as t:
                    cf = Chain(chain_f)
                    cf.turn((L * ((FC - 1) // 3) + t) * CHAIN_F, CHAIN_F)
                    for k in range(3):
                        i = t * 3 + (k + 1)
                        up(i, None, cf, L * (2 * GROUPS) + t * 12 + (2 * U0 + 4 * (k + 1) + 2),
                           L * TILES + t * 6 + (TU0 + 2 * (k + 1) + 2))
                    cf.end()

                dve.wait_ge(vec_ready, L * 16 + 32)
                dve.wait_ge(act_ready, 1 + L * FC + FC)
                ve.memset(ssq[:, :], 0.0).then_inc(ssq_zero, 1)
                dve.wait_ge(ssq_zero, L + 1)
                alone(dve)
                with dve.Fori(0, DC // 2) as t:
                    cd = Chain(chain_d)
                    cd.turn((L * (DC // 2) + t) * CHAIN_D, CHAIN_D)
                    current[0] = cd
                    for k in range(2):
                        c = t * 2 + k
                        x_c = x[:, bass.ds(c, 1), :]
                        a3 = acc[k][:, :].unsqueeze(1)
                        dve.wait_ge(halves, 1 + L * (2 * GROUPS) + t * (4 * DG) + (2 * D0 + 2 * DG * (k + 1)))
                        ve.scalar_tensor_tensor(out=x_c, in0=a3, scalar=0.5, in1=x_c,
                                                op0=ALU.mult, op1=ALU.add).then_inc(acc_free, 1)
                        dve.wait_ge(acc_free, 1 + L * TILES + t * 2 + (TD0 + k + 2))
                        split_x(c, vc_[:, bass.ds(c + VEC["norm1"], 1)], x_c,
                                xg_hi[:, bass.ds(c, 1), :], xg_lo[:, bass.ds(c, 1), :])
                        add_square(2 + k, L * 16 + t * 2 + (SSQ0 + DC + k + 1), None)
                    cd.end()

            dve.wait_ge(root_ready, 2 * LAYERS + 1)
            ve.reciprocal(rstd[:, :], rstd[:, :]).then_inc(s_free, 1)
            dve.wait_ge(s_free, 1 + LAYERS * len(S_USES) + 2)
            for c in range(DC):
                ve.scalar_tensor_tensor(out=x[:, c, :], in0=x[:, c, :], scalar=V("norm1", c), in1=rstd[:, :],
                                        op0=ALU.mult, op1=ALU.mult).then_inc(y_ready, 1)

        @block.tensor
        def _(pe):
            mm = nc.tensor.matmul
            used = {"s": 0, "t": 0}
            pe.sem_inc(halves, 1)

            def product(tile, slot, chunk, right_hi, right_lo, first, last):
                w_h, w_l = (w[:, slot, chunk * P:(chunk + 1) * P] for w in (w_hi, w_lo))
                mm(tile, w_h, right_hi, start=first, stop=False)
                mm(tile, w_h, right_lo, start=False, stop=False)
                return mm(tile, w_l, right_hi, start=False, stop=last)

            with pe.Fori(0, LAYERS) as L:
                used.update(s=0, t=0)

                def group_here(g, loop=None, per=0):
                    v = L * GROUPS + (g + 1)
                    if loop is not None:
                        v = v + loop * per
                    pe.wait_ge(hi_ready, v)
                    pe.wait_ge(lo_ready, 1 + v)

                def tile_free(T, loop=None, per=0):
                    v = L * TILES + T
                    if loop is not None:
                        v = v + loop * per
                    pe.wait_ge(acc_free, 1 + v)

                def quarter(g, q, tile, wait=False):
                    for c in (2 * q, 2 * q + 1):
                        if wait:
                            pe.wait_ge(xg_ready, L * 16 + (c + 1 + wait - 1))
                        ins = product(tile[:, :], g % RING, c, xg_hi[:, c, :], xg_lo[:, c, :], c == 0, c == CH - 1)
                    if q % 2:
                        ins.then_inc(halves, 1)

                def projection(g, tile, wait=False, norm=None):
                    for q in range(4):
                        quarter(g, q, tile, wait)
                        if norm and q == 2:
                            sum_squares(*norm)

                def s_begin(name):
                    used["s"] += 1
                    assert S_USES.index(name) + 1 == used["s"], name
                    pe.wait_ge(s_free, 1 + L * len(S_USES) + S_USES.index(name))
                    return s_of(name)

                def t_begin(name):
                    used["t"] += 1
                    assert T_USES.index(name) + 1 == used["t"], name
                    pe.wait_ge(t_free, 1 + L * len(T_USES) + T_USES.index(name))
                    return t_of(name)

                def last_wait():
                    pe.wait_ge(con_ready, 16)

                def sum_squares(use, value):
                    pe.wait_ge(ssq_ready, value)
                    b = s_begin(use)
                    last_wait()
                    mm(b[:, :], ones, ssq[:, :], start=True, stop=True).then_inc(s_done, 1)

                def compress(kind, w1_, win, i):
                    pe.wait_ge(v_made, v_count(L, f"win_{kind}"))
                    pe.wait_ge(w1_ready[i], L * 16 + 16)
                    b = s_begin(f"hid_{kind}")
                    last_wait()
                    for l in range(BLOCK):
                        ins = mm(b[:, 0:NCMP], w1_[:, l, :], win[:, l, :], start=(l == 0), stop=(l == BLOCK - 1))
                    ins.then_inc(s_done, 1)

                def turn4(name, src):
                    b = t_begin(name)
                    last_wait()
                    for k in range(QT):
                        ins = nc.tensor.transpose(b[:, k * P:(k + 1) * P], src[:, k * P:(k + 1) * P], ident)
                    ins.then_inc(t_done, 1)

                for g, name in enumerate(A_TILES):
                    group_here(g)
                    tile_free(g)
                    if name == "pad":
                        for _ in range(2):
                            mm(acc[1][:, 0:2], w_hi[:, g % RING, 0:P], xg_hi[:, 0, 0:2], start=True, stop=True).then_inc(halves, 1)
                    else:
                        projection(g, acc[g % 2], wait=1 if g == 0 else False,
                                   norm=("sumsq1", L * 16 + DC) if g == 0 else None)
                    if g == 4:
                        compress("k", w1k, win_k, 0)
                    if g == 6:
                        compress("v", w1v, win_v, 1)
                    if g == 7:
                        pe.wait_ge(v_made, v_count(L, "hid_k"))
                        b = s_begin("kc")
                        last_wait()
                        mm(b[:, 0:NCMP], V("w2k", 0, P), hid, start=True, stop=True).then_inc(s_done, 1)
                    if g == 9:
                        pe.wait_ge(v_made, v_count(L, "hid_v"))
                        b = s_begin("vc")
                        last_wait()
                        mm(b[0:NCMP, 0:P], hid, V("w2v", 0, P), start=True, stop=True).then_inc(s_done, 1)
                        b = s_begin("kc_swap")
                        pe.wait_ge(s_free, 1 + s_use(L, "kc") + 1)
                        last_wait()
                        mm(b[:, 0:NCMP], swap, kc[:, 0:NCMP], start=True, stop=True).then_inc(s_done, 1)
                    if g in (5, 7):
                        i = (g - 5) // 2
                        pe.wait_ge(acc_free, 1 + L * TILES + (4 + i + 2))
                        turn4(("v_slc", "v_win")[i], sc[:, i, :])

                def gate(e):
                    pe.wait_ge(a_made, a_count(L, "gate"))
                    b = s_begin(e)
                    alone(pe)
                    for k in range(QT):
                        ins = nc.tensor.transpose(b[:, k * P:k * P + 32], sc[0:32, 2, k * P:(k + 1) * P], ident[0:32, 0:32])
                    ins.then_inc(s_done, 1)

                def cmp_scores(e):
                    qi = e[1]
                    if qi == 0:
                        pe.wait_ge(v_made, v_count(L, "kc"))
                    b = s_begin(e)
                    last_wait()
                    for h in range(HEADS):
                        r = slice(64 * (h // 4), 64 * (h // 4) + 64)
                        ins = mm(b[:, 32 * h:32 * h + NCMP], qT[r, h % 4, qi * P:(qi + 1) * P], kc[r, 0:NCMP], start=True, stop=True)
                        if h == 3:
                            ins.then_inc(rows_done, 1)
                            pe.wait_ge(rows_done, L * QT + (qi + 1))
                    ins.then_inc(s_done, 1)

                def scores(e):
                    qi, br, h = unit(e[1])
                    w = (qi + 1) * P
                    r = slice(64 * (h // 4), 64 * (h // 4) + 64)
                    if e[1] < 2:
                        pe.wait_ge(v_made, v_count(L, "q0"))
                    b = s_begin(e)
                    last_wait()
                    mm(b[:, 0:w], qT[r, h % 4, qi * P:(qi + 1) * P], kT[r, br, 0:w], start=True, stop=True).then_inc(s_done, 1)

                def turn(e):
                    u = e[1]
                    pe.wait_ge(a_made, a_count(L, ("scores", u)))
                    b = t_begin(e)
                    last_wait()
                    for k in range(unit(u)[0] + 1):
                        ins = nc.tensor.transpose(b[:, k * P:(k + 1) * P], pr[:, u % 2, k * P:(k + 1) * P], ident)
                    ins.then_inc(t_done, 1)

                def values(e):
                    u = e[1]
                    qi, br, h = unit(u)
                    pe.wait_ge(t_free, 1 + t_use(L, ("turn", u)) + 1)
                    if u % 8 == 0:
                        pe.wait_ge(o_free, 1 + L * (2 * QT + RH) + (2 * qi + br))
                    last_wait()
                    for k in range(qi + 1):
                        ins = mm(o_bank[br][:, h * DH:(h + 1) * DH], pT[:, u % 2, k * P:(k + 1) * P],
                                 v_nat[:, br, k, 64 * (h // 4):64 * (h // 4) + 64], start=(k == 0), stop=(k == qi))
                    ins.then_inc(pv_done, 1)

                def cmp_turn(e):
                    pe.wait_ge(a_made, a_count(L, ("cmp_scores", e[1])))
                    for half in range(2):
                        b = t_begin((*e, half))
                        last_wait()
                        for i in range(4):
                            ins = nc.tensor.transpose(b[0:NCMP, i * P:(i + 1) * P], cmp_p[:, 4 * half + i, :], ident)
                        ins.then_inc(t_done, 1)

                def cmp_values(e):
                    pe.wait_ge(t_free, 1 + t_use(L, ("cmp_turn", e[1], 1)) + 1)
                    b = s_begin(e)
                    last_wait()
                    for h in range(HEADS):
                        ins = mm(b[:, h * DH:(h + 1) * DH], cmp_pT[0:NCMP, h // 4, h % 4 * P:(h % 4 + 1) * P],
                                 vc[0:NCMP, 64 * (h // 4):64 * (h // 4) + 64], start=True, stop=True)
                    ins.then_inc(s_done, 1)

                def mix_turn(e):
                    pe.wait_ge(v_made, v_count(L, ("mix", e[1])))
                    turn4(e, mixed[:, :])

                def ret_turn(e):
                    pe.wait_ge(acc_free, 1 + L * TILES + (A_GROUPS + B_TILES.index(("rv", e[1])) + 2))
                    turn4(e, rv_T[:, :])

                def ret_scores(e):
                    h, m = e[1], e[2]
                    if m == 0:
                        pe.wait_ge(v_made, v_count(L, ("rk", h)))
                    b = s_begin(e)
                    last_wait()
                    mm(b[:, 0:S - m * P], rk[:, h % 2, m * P:(m + 1) * P], rq[:, h % 2, m * P:S],
                       start=True, stop=True).then_inc(s_done, 1)

                def ret_values(e):
                    h, m = e[1], e[2]
                    pe.wait_ge(s_free, 1 + s_use(L, ("ret_scores", h, m)) + 1)
                    if m == 0:
                        pe.wait_ge(t_free, 1 + t_use(L, ("ret_turn", h)) + 1)
                        pe.wait_ge(o_free, 1 + L * (2 * QT + RH) + (2 * QT + h))
                    last_wait()
                    mm(o_bank[h % 2][:, m * P:S], rv[:, m, :], pr[:, m % 2, 0:S - m * P],
                       start=(m == 0), stop=(m == QT - 1)).then_inc(pv_done, 1)

                def ret_var(e):
                    pe.wait_ge(a_made, a_count(L, ("ret_values", e[1], QT - 1)))
                    b = s_begin(e)
                    last_wait()
                    mm(b[:, :], ones, pT[:, 1, :], start=True, stop=True).then_inc(s_done, 1)

                def pool(e):
                    g = e[1]
                    if g == 0:
                        pe.wait_ge(pool_w_ready, L * 16 + 16)
                    pe.wait_ge(v_made, v_count(L, ("u", g)))
                    b = s_begin(e)
                    last_wait()
                    mm(b[:, :], sc[:, 3, g * P:(g + 1) * P], pooled[g], start=True, stop=True).then_inc(s_done, 1)

                steps = {"gate": gate, "cmp_scores": cmp_scores, "scores": scores, "turn": turn, "values": values,
                         "cmp_turn": cmp_turn, "cmp_values": cmp_values, "mix_turn": mix_turn, "ret_scores": ret_scores,
                         "ret_values": ret_values, "ret_turn": ret_turn, "ret_var": ret_var, "pool": pool}

                for b in range(B_GROUPS):
                    g = A_GROUPS + b
                    group_here(g)
                    tile_free(g)
                    for q in range(4):
                        quarter(g, q, acc[g % 2])
                        for e in SIDE[4 * b + q]:
                            if e[0] in steps:
                                steps[e[0]](e)

                with pe.Fori(0, DC) as j:
                    for n in range(4):
                        group_here(J0 + n, j, J_GROUPS)
                        tile_free(TJ0 + n, j, 8)
                        projection(J0 + n, acc[n % 2])
                    for n in range(4):
                        g = J0 + 4 + n // 2
                        if n % 2 == 0:
                            group_here(g, j, J_GROUPS)
                        tile_free(TJ0 + 4 + n, j, 8)
                        if n == 0:
                            pe.wait_ge(v_made, v_count(L, "branches"))
                        for c in range(BC):
                            ins = product(acc[n % 2][:, :], g % RING, BC * (n % 2) + c, y_hi[n][:, c, :], y_lo[n][:, c, :],
                                          c == 0, c == BC - 1)
                        ins.then_inc(halves, 1)

                for j in range(DC):
                    g, T = O0 + j, TO0 + j
                    group_here(g)
                    tile_free(T)
                    for c in range(DC):
                        if j == 0:
                            pe.wait_ge(mrg_ready, 1 + L * DC + (c + 1))
                        ins = product(acc[T % 2][:, :], g % RING, c, mrg_hi[:, c, :], mrg_lo[:, c, :], c == 0, c == DC - 1)
                        if c % 4 == 3:
                            ins.then_inc(halves, 1)

                for k in range(2):
                    group_here(U0 + k)
                    tile_free(TU0 + k)
                    projection(U0 + k, acc[k], wait=DC + 1 if k == 0 else False,
                               norm=("sumsq2", L * 16 + 2 * DC) if k == 0 else None)
                assert used == {"s": len(S_USES), "t": len(T_USES)}
                with pe.Fori(0, (FC - 1) // 3) as t:
                    for k in range(6):
                        group_here(U0 + 2 + k, t, 6)
                        tile_free(TU0 + 2 + k, t, 6)
                        projection(U0 + 2 + k, acc[k % 2])

                with pe.Fori(0, DC // 2) as t:
                    for k in range(2):
                        tile_free(TD0 + k, t, 2)
                        for c in range(FC):
                            g = D0 + DG * k + c // CH
                            if c % CH == 0:
                                group_here(g, t, 2 * DG)
                            if c == 0:
                                pe.wait_ge(act_ready, 1 + L * FC + (FC - 1))
                            if c == FC - 1:
                                pe.wait_ge(act_ready, 1 + L * FC + FC)
                            ins = product(acc[k][:, :], g % RING, c % CH, act_hi[:, c, :], act_lo[:, c, :], c == 0, c == FC - 1)
                            if c % 4 == 3 or c == FC - 1:
                                ins.then_inc(halves, 1)

            pe.wait_ge(ssq_ready, LAYERS * 16 + DC)
            pe.wait_ge(s_free, 1 + LAYERS * len(S_USES))
            mm(s_bank[0][:, :], ones, ssq[:, :], start=True, stop=True).then_inc(s_done, 1)


CHAIN_LAYER, CHAIN_J, CHAIN_F, CHAIN_D = 171, 4, 15, 2


def _constants():
    con = np.zeros((P, NCON), np.float32)

    def put(name, a):
        con[0:a.shape[0], CON[name]:CON[name] + a.shape[1]] = a

    put("ident", np.eye(P, dtype=np.float32))
    swap = np.zeros((P, P), np.float32)
    for o in (0, 64):
        for i in range(8):
            swap[o + i, o + 8 + i] = swap[o + 8 + i, o + i] = 1
    put("swap", swap)
    put("ones", np.ones((P, P), np.float32))
    p, f = np.arange(P)[:, None], np.arange(S)[None, :]
    put("causal", np.where(f - (S - P) > p, NEG, 0).astype(np.float32))
    ends = np.arange(NCMP) * STRIDE + BLOCK - 1
    for qi in range(QT):
        m = np.where(ends[None, :] <= qi * P + p, 0, NEG).astype(np.float32)
        con[:, CON["cmp_mask"] + qi * NCMP:CON["cmp_mask"] + (qi + 1) * NCMP] = m
    put("seen", (p >= BLOCK - 1).astype(np.float32))
    con[:, CON["eps"]] = EPS

    def angles(theta, half, pos):
        inv = np.power(np.float32(theta), -np.arange(half, dtype=np.float32) / np.float32(half))
        a = (pos.astype(np.float32)[None, :] * inv[:, None]).astype(np.float32)
        return np.cos(a).astype(np.float32), np.sin(a).astype(np.float32)

    for suffix, pos in (("a", np.arange(S)), ("c", ends)):
        c, s = angles(500000.0, 8, pos)
        cos, sin = np.ones((P, len(pos)), np.float32), np.zeros((P, len(pos)), np.float32)
        for o in (0, 64):
            cos[o:o + 8], cos[o + 8:o + 16] = c, c
            sin[o:o + 8], sin[o + 8:o + 16] = -s, s
        put(f"cos_{suffix}", cos)
        put(f"sin_{suffix}", sin)
    c, s = angles(10000.0, RD // 2, np.arange(S))
    put("cos_r", np.concatenate([c, c]))
    put("sin_r", np.concatenate([-s, s]))
    for g, n in enumerate(POOLS):
        con[:, CON["pool_fix"] + 16 * g:CON["pool_fix"] + 16 * g + n - 1] = n / np.arange(1, n, dtype=np.float32)
    log_g = np.log1p(-np.exp2(-5.0 - np.arange(RH)))
    diff = (f - p)[None]
    dec = np.where(diff >= 0, np.exp(np.maximum(diff, 0) * log_g[:, None, None]), 0) * RD ** -0.5
    return con, dec.astype(np.float32)


def _tiles(w):
    k, m = w.shape
    return w.reshape(k // P, P, m // P, P).transpose(2, 1, 0, 3)


def _weights(w_in, w_branch, w_o, w_up, w_down):
    at = np.cumsum([0, 3 * BW, HEADS * DH, 3 * 2 * KV_GROUPS * DH, 3 * HEADS, 4 * BW, BW])
    z_sc, z_q, z_kv, z_ng, z_ret, z_pool, z_gate = (w_in[:, a:b] for a, b in zip(at, [*at[1:], w_in.shape[1]]))
    kv = _tiles(z_kv)
    q = z_q.reshape(D, 2, 4, DH).transpose(0, 2, 1, 3).reshape(D, HEADS * DH)
    ng = np.zeros((D, P), np.float32)
    ng[:, 0:3 * HEADS] = z_ng
    a = [kv[0], kv[1], kv[2], kv[4], kv[3], kv[5], *_tiles(q), _tiles(ng)[0], np.zeros((P, CH, P), np.float32)]
    ret, sc, pool = _tiles(z_ret), _tiles(z_sc), _tiles(z_pool)
    part = {"rq": (ret, 0), "rk": (ret, 4), "rv": (ret, 8), "rg": (ret, 12), "b": (sc, 0), "c": (sc, 4), "h": (sc, 8), "u": (pool, 0)}
    b = [part[k][0][part[k][1] + i] for k, i in B_TILES]
    gate, branch = _tiles(z_gate), [_tiles(w) for w in w_branch]
    js = []
    for j in range(DC):
        js += [gate[n * DC + j] for n in range(4)]
        js += [np.concatenate([branch[n][j], branch[n + 1][j]], axis=1) for n in (0, 2)]
    up = _tiles(w_up)
    ups = [up[k * FC + i] for i in range(FC) for k in range(2)]
    down = np.zeros((DC, P, DG * CH, P), np.float32)
    down[:, :, 0:FC] = _tiles(w_down)
    downs = [down[j, :, CH * m:CH * (m + 1)] for j in range(DC) for m in range(DG)]
    return np.stack([*a, *b, *js, *_tiles(w_o), *ups, *downs]).reshape(GROUPS, P, CH * P)


def kernel(**inputs):
    import concourse.bacc as bacc
    from concourse.bass_utils import run_bass_kernel_spmd

    i = {k: np.asarray(v) for k, v in inputs.items()}
    arrays = {"xT": np.ascontiguousarray(i["x"][0].T.reshape(DC, P, S).transpose(1, 0, 2))}
    groups = [_weights(*(i[k][l] for k in ("w_in", "w_branch", "w_o", "w_up", "w_down"))) for l in range(LAYERS)]
    arrays["weights"] = np.concatenate([*groups, np.zeros((RING, P, CH * P), np.float32)])

    def cols(a, n):
        return a.reshape(-1, n, P).transpose(2, 1, 0).reshape(P, -1)

    def diagonal(w):
        out = np.zeros((P, *w.shape[:-2], P), np.float32)
        for g in range(KV_GROUPS):
            out[g * DH:(g + 1) * DH, ..., g * DH:(g + 1) * DH] = np.moveaxis(w, -2, 0)
        return out

    vec = np.zeros((LAYERS + 1, P, NVEC), np.float32)
    for l in range(LAYERS):
        parts = {"norm1": cols(i["norm1_g"][l], DC), "norm2": cols(i["norm2_g"][l], DC), "b_gate": cols(i["b_gate"][l], 4 * DC),
                 "sc_conv": cols(i["sc_conv"][l], BC), "ret_gn": cols(i["ret_gn_g"][l], BC),
                 "pool_scale": cols(i["pool_scale"][l], BC), "ffn_conv": cols(i["ffn_conv"][l], FC),
                 "pe": np.concatenate([i["cmp_pe"][l].T] * KV_GROUPS), "w2k": diagonal(i["cmp_w2_k"][l]),
                 "w2v": diagonal(i["cmp_w2_v"][l])}
        for name, a in parts.items():
            vec[l, :, VEC[name]:VEC[name] + a.shape[1]] = a
    vec[LAYERS, :, 0:DC] = cols(i["final_norm_g"], DC)
    arrays["vec"] = vec
    arrays["w1"] = np.stack([diagonal(i[k][l]) for l in range(LAYERS) for k in ("cmp_w1_k", "cmp_w1_v")])
    arrays["pool_w"] = np.ascontiguousarray(i["pool_w"].transpose(0, 2, 1, 3))
    arrays["consts"], arrays["decay"] = _constants()

    nc = bacc.Bacc("TRN2", target_bir_lowering=False, num_devices=1)
    args = [nc.dram_tensor(f"{n}_dram", a.shape, F32, kind="ExternalInput").ap() for n, a in arrays.items()]
    out = nc.dram_tensor("out_dram", (P, DC, S), F32, kind="ExternalOutput").ap()
    build(nc, *args, out)
    r = run_bass_kernel_spmd(nc, [{f"{n}_dram": a for n, a in arrays.items()}], core_ids=[0])
    y = np.asarray(r.results[0]["out_dram"])
    return y.transpose(1, 0, 2).reshape(D, S).T.reshape(1, S, D)
```

```python
from contextlib import ExitStack

import numpy as np

import concourse.bass as bass
from concourse import mybir

F32 = mybir.dt.float32
F32R = mybir.dt.float32r
ALU = mybir.AluOpType
ACT = mybir.ActivationFunctionType
AX = mybir.AxisListType

P = 128
S = 512
D = 1024
DC = D // P
LAYERS = 2
BW = 512
BC = BW // P
FF = 2816
FC = FF // P
HEADS, KV_GROUPS, DH = 8, 2, 64
BLOCK, STRIDE = 32, 16
NCMP = (S - BLOCK) // STRIDE + 1
RH, RD = 4, 128
POOLS = (2, 4, 8, 16)
EPS = 1e-6
NEG = -1e30
QT = S // P

CH = 8
RING = 3
A_GROUPS = 12
B_GROUPS = 32
J_GROUPS = 6
J0 = A_GROUPS + B_GROUPS
O0 = J0 + DC * J_GROUPS
U0 = O0 + DC
D0 = U0 + 2 * FC
DG = 3
GROUPS = D0 + DC * DG
assert GROUPS % RING == 0 and J_GROUPS % RING == 0
TJ0 = J0
TO0 = TJ0 + DC * 8
TU0 = TO0 + DC
TD0 = TU0 + 2 * FC
TILES = TD0 + DC
assert TILES % 2 == 0

A_TILES = ["k_cmp", "v_cmp", "k_slc", "k_win", "v_slc", "v_win", "q0", "q1", "q2", "q3", "gate", "pad"]
RET0 = [0, 16, 20, 24]
SC0 = [4, 7, 10, 29]
RET_SLOT = [68, 80, 96, 112]
POOL0 = [28, 13, 14, 15]
POOL_SLOT = [127, 85, 101, 117]
B_TILES = [None] * B_GROUPS
for _h in range(RH):
    B_TILES[RET0[_h]:RET0[_h] + 4] = [("rq", _h), ("rk", _h), ("rv", _h), ("rg", _h)]
for _j in range(BC):
    B_TILES[SC0[_j]:SC0[_j] + 3] = [("c", _j), ("h", _j), ("b", _j)]
    B_TILES[POOL0[_j]] = ("u", _j)

UNITS = 2 * QT * HEADS
SLOTS = 4 * B_GROUPS
SIDE = [[] for _ in range(SLOTS)]
UNIT_SLOT = 4
for _n in range(UNITS + 4):
    _e, _qi = SIDE[UNIT_SLOT + _n], _n // 16
    if _n < UNITS and _n % 16 == 0:
        _e.append(("cmp_scores", _qi))
    if _n < UNITS and _n % 16 == 2:
        _e.append(("cmp_scale", _qi))
    if _n < UNITS and _n % 16 == 4:
        _e.append(("cmp_turn", _qi))
    if _n % 2 == 0 and _n < UNITS:
        _e += [("scores", _n), ("scores", _n + 1)]
    if _n % 2 and _n < UNITS:
        _e.append(("scale", _n - 1))
    if _n % 2 and _n >= 5:
        _e.append(("values", _n - 5))
    if _n % 2 and 3 <= _n < UNITS + 2:
        _e += [("turn", _n - 3), ("turn", _n - 2)]
for _h in range(RH):
    _n0 = RET_SLOT[_h]
    for _m in range(QT):
        SIDE[_n0 + _m].append(("ret_scores", _h, _m))
        SIDE[_n0 + _m + 1].append(("ret_values", _h, _m))
    SIDE[_n0 + 5].append(("ret_gate", _h))
    SIDE[_n0 + 6].append(("ret_var", _h))
    SIDE[_n0 + 7].append(("ret_inverse", _h))
    SIDE[POOL_SLOT[_h]].append(("pool", _h))
for _h in range(RH):
    SIDE[RET_SLOT[_h] + (8, 8, 8, 12)[_h]].append(("ret_end", _h))
    SIDE[RET_SLOT[_h] + (14, 12, 12, 14)[_h]].append(("ret_split", _h))
    SIDE[4 * (RET0[_h] + 3) + 3].append(("ret_turn", _h))
SIDE[2].append(("gate",))
for _b in range(B_GROUPS - 1):
    for _k in range(4):
        if B_TILES[_b][0] == "b":
            SIDE[4 * (_b + 1) + _k].append(("conv", B_TILES[_b][1], _k))
        if B_TILES[_b][0] == "u":
            SIDE[4 * (_b + 1) + _k].append(("mean", B_TILES[_b][1], _k))
        if B_TILES[_b][0] in ("rq", "rk") and _k < 2:
            SIDE[4 * (_b + 2) + 1 + _k].append(("rotate", B_TILES[_b], _k))
SEQUENCE = [_e for _slot in SIDE for _e in _slot]

S_USES = ["sumsq1", "hid_k", "hid_v", "kc", "vc", "kc_swap"]
S_USES += [_e for _e in SEQUENCE if _e[0] in ("gate", "cmp_scores", "scores", "ret_scores", "ret_var", "pool")]
S_USES += ["sumsq2"]
T_USES = ["v_slc", "v_win"]
for _e in SEQUENCE:
    if _e[0] in ("turn", "ret_turn"):
        T_USES.append(_e)
    if _e[0] == "cmp_turn":
        T_USES += [(*_e, 0), (*_e, 1)]
assert len(S_USES) % 2 == 0 and len(T_USES) % 2 == 0
V_MADE = ["win_k", "win_v", "k0", "k1", "arg_k", "hid_k", "q0", "arg_v", "q1", "hid_v", "q2", "q3", "kc"]
A_MADE = ["hid_k", "hid_v", "gate"]
for _slot in SIDE:
    for _e in _slot:
        if _e[0] in ("cmp_scores", "scores", "ret_gate", "ret_var") or _e[0] == "ret_values" and _e[2] == QT - 1:
            A_MADE.append(_e)
        if _e[0] == "scale":
            A_MADE += [_e, ("scale", _e[1] + 1)]
        if _e[0] in ("cmp_scores", "cmp_scale", "scale"):
            V_MADE.append(_e)
        if _e[0] == "mean" and _e[2] == 3:
            V_MADE.append(("u", _e[1]))
        if _e[0] == "rotate" and _e[2] == 1:
            V_MADE.append(_e[1])
V_MADE.append("branches")
PV_MADE = [_x for _e in SEQUENCE for _x in ([_e, ("values", _e[1] + 1)] if _e[0] == "values" else [_e] if _e[0] == "ret_values" else [])]
OUTS = QT + RH

def _columns(parts):
    at, out = 0, {}
    for name, n in parts:
        out[name] = at
        at += n
    return out, at


VEC, NVEC = _columns([("norm1", DC), ("norm2", DC), ("b_gate", 4 * DC), ("sc_conv", 3 * BC), ("ret_gn", BC),
                      ("pool_scale", BC), ("ffn_conv", 3 * FC), ("pe", BLOCK), ("w2k", DH), ("w2v", DH)])
CON, NCON = _columns([("ident", P), ("swap", P), ("ones", P), ("causal", S), ("cmp_mask", QT * NCMP), ("seen", 1),
                      ("eps", 1), ("cos_a", S), ("sin_a", S), ("cos_c", NCMP), ("sin_c", NCMP), ("cos_r", S),
                      ("sin_r", S), ("pool_fix", 16 * 4)])


def build(nc, xT, weights, vec, w1, pool_w, consts, decay, out):
    with ExitStack() as ctx:
        sem = lambda name: ctx.enter_context(nc.semaphore(name))

        KB = 1024
        base = (nc.sbuf_base + 127) // 128 * 128

        def at(name, shape, dt, offset):
            n = 4 * int(np.prod(shape[1:]))
            assert base + offset + n <= nc.sbuf_usable_end, (name, offset)
            return nc.alloc_sbuf_tensor_at(name, shape, dt, offset=base + offset)

        x = at("x", [P, DC, S], F32, 0)
        xg_hi = at("xg_hi", [P, DC, S], F32R, 16 * KB)
        xg_lo = at("xg_lo", [P, DC, S], F32R, 32 * KB)
        w_raw = at("w_raw", [P, RING, CH * P], F32, 48 * KB)
        w_hi = at("w_hi", [P, RING, CH * P], F32R, 60 * KB)
        w_lo = at("w_lo", [P, RING, CH * P], F32R, 72 * KB)
        Y = 84 * KB
        y_hi = [at(f"y_hi{n}", [P, BC, S], F32R, Y + n * 16 * KB) for n in range(4)]
        y_lo = [at(f"y_lo{n}", [P, BC, S], F32R, Y + n * 16 * KB + 8 * KB) for n in range(4)]
        qT = at("qT", [P, 4, S], F32, Y + 48 * KB)
        kT = at("kT", [P, 2, S], F32, Y + 56 * KB)
        v_nat = at("v_nat", [P, 2, QT, P], F32, Y + 60 * KB)
        w1v = at("w1v", [P, BLOCK // 2, DH], F32, Y + 32 * KB)
        pr_odd = at("pr_odd", [P, 2, S], F32, Y + 32 * KB)
        cmp_pT = at("cmp_pT", [P, 2, S], F32, Y + 36 * KB)
        cmp_p = at("cmp_p", [P, HEADS, NCMP], F32, Y + 40 * KB)
        kc = at("kc", [P, 32], F32, Y + 41 * KB)
        kc_rot = at("kc_rot", [P, 32], F32, Y + 41 * KB + 128)
        vc = at("vc", [32, P], F32, Y + 41 * KB + 256)
        W = Y + 64 * KB
        w1k = at("w1k", [P, BLOCK // 2, DH], F32, W)
        rq = at("rq", [P, 2, S], F32, W)
        rk = at("rk", [P, 2, S], F32, W + 4 * KB)
        rv = at("rv", [P, QT, P], F32, W + 8 * KB)
        rv_T = at("rv_T", [P, S], F32, W + 10 * KB)
        rg = at("rg", [P, S], F32, W + 12 * KB)
        rg_t = at("rg_t", [P, S], F32, W + 14 * KB)
        sc = at("sc", [P, 4, S], F32, W + 16 * KB)
        pool_early = at("pool_early", [P, 3, S], F32, Y + 42 * KB)
        rot = at("rot", [P, 2, S], F32, W + 24 * KB)
        pooled = [rot[:, 0, :], pool_early[:, 0, :], pool_early[:, 1, :], pool_early[:, 2, :]]
        dec = at("dec", [P, 2, S], F32, W + 28 * KB)
        k_cmp = at("k_cmp", [P, S], F32, W + 28 * KB)
        v_cmp = at("v_cmp", [P, S], F32, W + 30 * KB)
        mrg_hi = at("mrg_hi", [P, DC, S], F32R, W)
        mrg_lo = at("mrg_lo", [P, DC, S], F32R, W + 16 * KB)
        act_hi = at("act_hi", [P, FC, S], F32R, Y)
        act_lo = at("act_lo", [P, FC, S], F32R, Y + 44 * KB)
        first_sq = at("first_sq", [P, DC, S], F32, Y)
        R = W + 32 * KB
        pr = at("pr", [P, 2, S], F32, R)
        pT = at("pT", [P, 2, S], F32, R + 4 * KB)
        win_k = at("win_k", [P, BLOCK // 2, KV_GROUPS * NCMP], F32, R)
        win_v = at("win_v", [P, BLOCK // 2, KV_GROUPS * NCMP], F32, R + 4 * KB)
        work = at("work", [P, 4, S], F32, R)
        rstd = at("rstd", [P, S], F32, R + 8 * KB)
        ssq = at("ssq", [P, S], F32, R + 10 * KB)
        R2 = R + 12 * KB
        con = at("con", [P, NCON], F32, R2)
        R3 = R2 + (4 * NCON + 31) // 32 * 32
        vc_ = at("vec", [P, NVEC], F32, R3)
        R4 = R3 + (4 * NVEC + 31) // 32 * 32
        gates = at("gates", [P, QT, 3 * HEADS], F32, R4)
        small = at("small", [P, 224], F32, R4 + 4 * QT * 3 * HEADS)
        hid = small[0:DH, 0:KV_GROUPS * NCMP]
        hid_a = small[0:DH, 152:152 + KV_GROUPS * NCMP]
        den = small[:, 64:68]
        scl = small[:, 68:72]
        nmax = small[:, 80:82]
        c_max = small[:, 82:90]
        c_den = small[:, 90:98]
        scale8 = small[:, 98:106]
        v_sum = small[:, 106:110]
        half_b = small[:, 112:144]
        pad_out = small[:, 144:146]

        def C(name, n, rows=P):
            return con[0:rows, CON[name]:CON[name] + n]

        def V(name, i=0, n=1):
            return vc_[:, VEC[name] + i:VEC[name] + i + n]

        ident, swap, ones = C("ident", P), C("swap", P), C("ones", P)

        bank = lambda name: ctx.enter_context(nc.psum_tensor(name, [P, S], F32))
        acc = [bank(f"acc{i}") for i in range(2)]
        s_bank = [bank(f"s{i}") for i in range(2)]
        t_bank = [bank(f"t{i}") for i in range(2)]
        o_bank = [bank(f"o{i}") for i in range(2)]

        raw_ready = [sem(f"raw_ready{i}") for i in range(RING)]
        hi_ready = sem("hi_ready")
        lo_ready = sem("lo_ready")
        halves = sem("halves")
        acc_free = sem("acc_free")
        s_done, s_free = sem("s_done"), sem("s_free")
        t_done, t_free = sem("t_done"), sem("t_free")
        pv_done, o_free = sem("pv_done"), sem("o_free")
        con_ready = sem("con_ready")
        vec_ready = sem("vec_ready")
        w1_ready = [sem("w1k_ready"), sem("w1v_ready")]
        x_in = [sem(f"x_in{c}") for c in range(DC)]
        pool_w_ready = sem("pool_w_ready")
        dec_ready = [sem("dec_ready0"), sem("dec_ready1")]
        rot_ready = [sem("rot_ready0"), sem("rot_ready1")]
        v_made = sem("v_made")
        a_made = sem("a_made")
        xg_ready = sem("xg_ready")
        ssq_ready = sem("ssq_ready")
        sq_ready = sem("sq_ready")
        root_ready = sem("root_ready")
        ssq_zero = sem("ssq_zero")
        tanh_ready = sem("tanh_ready")
        mrg_ready = sem("mrg_ready")
        conv_ready = sem("conv_ready")
        silu_ready = sem("silu_ready")
        act_ready = sem("act_ready")
        y_ready = sem("y_ready")
        stored = sem("stored")
        rows_done = sem("rows_done")
        passed = sem("passed")
        chain = sem("chain")
        chain_j, chain_f, chain_d = sem("chain_j"), sem("chain_f"), sem("chain_d")

        def s_use(L, name):
            return L * len(S_USES) + S_USES.index(name) + 1

        def t_use(L, name):
            return L * len(T_USES) + T_USES.index(name) + 1

        def v_count(L, name):
            return L * len(V_MADE) + V_MADE.index(name) + 1

        def a_count(L, name):
            return L * len(A_MADE) + A_MADE.index(name) + 1

        def pv_count(L, name):
            return L * len(PV_MADE) + PV_MADE.index(name) + 1

        def s_of(name):
            return s_bank[S_USES.index(name) % 2]

        def t_of(name):
            return t_bank[T_USES.index(name) % 2]

        ROT = {n: i for i, n in enumerate(["k0", "k1", "q0", "q1", "q2", "q3"])}
        for h in range(RH):
            ROT[("rq", h)], ROT[("rk", h)] = 6 + 2 * h, 7 + 2 * h
        ROT_DMA = 16 * (3 * 4 + RH * 2)

        def rot_value(L, name):
            i = ROT[name] // 2
            return L * ROT_DMA + 16 * (4 * (i + 1) if i < 3 else 12 + 2 * (i - 2))

        A_AT = {"k0": 2, "k1": 3, "q0": 6, "q1": 7, "q2": 8, "q3": 9}

        def alone(engine):
            engine.sem_inc(passed, 1)

        def unit(u):
            return u // 16, u // 2 % 2, u % 16 // 4 + 4 * (u % 2)

        def pr_of(u):
            return (pr, pr_odd)[u // 2 % 2][:, u % 2, 0:(unit(u)[0] + 1) * P]

        block = ctx.enter_context(nc.Block())

        @block.sync
        def _(sp):
            def load_group(g, slot):
                sp.dma_start(w_raw[:, slot, :],
                             weights[bass.ds(g, 1), :, :].rearrange("a p n -> (a p) n")).then_inc(raw_ready[slot], 16)

            def load_groups(L, first, last):
                with sp.Fori(0, (last - first) // RING) as t:
                    for k in range(RING):
                        g = L * GROUPS + t * RING + (first + k)
                        sp.wait_ge(lo_ready, 1 + g - (RING - 1))
                        load_group(g + 0, (first + k) % RING)

            load_group(0, 0)
            sp.dma_start(vc_[:, :], vec[0, :, :]).then_inc(vec_ready, 16)
            sp.dma_start(x[:, 0, :], xT[:, 0, :]).then_inc(x_in[0], 16)
            for c in range(1, DC):
                sp.dma_start(x[:, c, :], xT[:, c, :]).then_inc(x_in[c], 16)
            load_group(1, 1)
            sp.dma_start(con[:, :], consts).then_inc(con_ready, 16)
            load_group(2, 2)
            with sp.Fori(0, LAYERS) as L:
                sp.wait_ge(halves, 1 + L * (2 * GROUPS))
                for k in range(RING):
                    g = RING + k
                    sp.wait_ge(lo_ready, 1 + L * GROUPS + (g - (RING - 1)))
                    load_group(L * GROUPS + g, g % RING)
                    if k < 2:
                        sp.dma_start((w1k, w1v)[k][:, :, :],
                                     w1[bass.ds(L * 2 + k, 1), :, :, :].rearrange("a p l n -> (a p) l n")).then_inc(w1_ready[k], 16)
                load_groups(L, 2 * RING, D0 + RING)
                sp.wait_ge(act_ready, 1 + L * FC + FC)
                sp.dma_start(vc_[:, :], vec[bass.ds(L + 1, 1), :, :].rearrange("a p n -> (a p) n")).then_inc(vec_ready, 16)
                load_groups(L, D0 + RING, GROUPS + RING)
            for c in range(DC):
                sp.wait_ge(y_ready, c + 1)
                sp.dma_start(out[:, c, :], x[:, c, :]).then_inc(stored, 16)
            sp.wait_ge(stored, 16 * DC)

        @block.gpsimd
        def _(pool):
            pool.sem_inc(lo_ready, 1)
            with pool.Fori(0, LAYERS * GROUPS // RING) as t:
                for k in range(RING):
                    pool.wait_ge(hi_ready, t * RING + (k + 1))
                    nc.gpsimd.tensor_tensor(w_lo[:, k, :], w_raw[:, k, :], w_hi[:, k, :].bitcast(F32),
                                            ALU.subtract).then_inc(lo_ready, 1)

        @block.scalar
        def _(act):
            def ahead(L, g, loop=None, per=0):
                at_g = L * (2 * GROUPS) + 2 * g
                turns = L * (16 * GROUPS // RING) + 16 * ((g + 2) // RING + 1)
                if loop is not None:
                    at_g = at_g + loop * (2 * per)
                    turns = turns + loop * (16 * per // RING)
                slot = (g + 2) % RING
                act.wait_ge(halves, 1 + at_g)
                act.wait_ge(raw_ready[slot], turns)
                nc.scalar.activation(w_hi[:, slot, :], w_raw[:, slot, :], ACT.Copy).then_inc(hi_ready, 1)

            def root(use, L):
                act.wait_ge(s_done, s_use(L, use))
                act.wait_ge(con_ready, 16)
                nc.scalar.activation(rstd[:, :], s_of(use)[:, :], ACT.Sqrt, bias=C("eps", 1),
                                     scale=1.0 / D).then_inc(root_ready, 1)

            def rotate_partners(L, name):
                i = ROT[name]
                dst = rot[:, i % 2, :]
                if isinstance(name, str):
                    act.wait_ge(acc_free, 1 + L * TILES + (A_AT[name] + 2))
                    if i >= 2:
                        before = [n for n, k in ROT.items() if k == i - 2][0]
                        act.wait_ge(v_made, v_count(L, before))
                    src = kT[:, int(name[1]), :] if name[0] == "k" else qT[:, int(name[1]), :]
                    for g in range(KV_GROUPS):
                        o = 64 * g
                        act.dma_start(dst[o:o + 8, :], src[o + 8:o + 16, :]).then_inc(rot_ready[i % 2], 16)
                        act.dma_start(dst[o + 8:o + 16, :], src[o:o + 8, :]).then_inc(rot_ready[i % 2], 16)
                else:
                    act.wait_ge(acc_free, 1 + L * TILES + (A_GROUPS + B_TILES.index(name) + 2))
                    before = [n for n, k in ROT.items() if k == i - 2][0]
                    act.wait_ge(v_made, v_count(L, before))
                    src = (rq if name[0] == "rq" else rk)[:, name[1] % 2, :]
                    act.dma_start(dst[0:64, :], src[64:128, :]).then_inc(rot_ready[i % 2], 16)
                    act.dma_start(dst[64:128, :], src[0:64, :]).then_inc(rot_ready[i % 2], 16)

            for c in range(DC):
                if c in (0, 4):
                    act.wait_ge(raw_ready[c // 4], 16)
                    nc.scalar.activation(w_hi[:, c // 4, :], w_raw[:, c // 4, :], ACT.Copy).then_inc(hi_ready, 1)
                act.wait_ge(x_in[c], 16)
                nc.scalar.activation(first_sq[:, c, :], x[:, c, :], ACT.Square).then_inc(sq_ready, 1)

            with act.Fori(0, LAYERS) as L:
                for g in range(A_GROUPS):
                    ahead(L, g)
                    if g == 2:
                        root("sumsq1", L)
                    for name in ("k0", "k1", "q0", "q1", "q2", "q3"):
                        if A_AT[name] == g - 1:
                            rotate_partners(L, name)
                    if g in (5, 8):
                        kind = "k" if g == 5 else "v"
                        act.wait_ge(v_made, v_count(L, f"arg_{kind}"))
                        nc.scalar.activation(hid_a, hid_a, ACT.Tanh, scale=0.7978845608028654).then_inc(a_made, 1)
                    if g == 11:
                        act.wait_ge(acc_free, 1 + L * TILES + 12)
                        nc.scalar.activation(sc[:, 2, :], sc[:, 2, :], ACT.Tanh, scale=0.5).then_inc(a_made, 1)

                for b in range(B_GROUPS):
                    ahead(L, A_GROUPS + b)
                    if 0 < b and B_TILES[b - 1][0] in ("rq", "rk"):
                        rotate_partners(L, B_TILES[b - 1])
                    for h in range(RH):
                        if b == 14 + 4 * h:
                            if h >= 2:
                                act.wait_ge(s_free, 1 + s_use(L, ("ret_scores", h - 2, QT - 1)) + 1)
                            act.dma_start(dec[:, h % 2, :], decay[h, :, :]).then_inc(dec_ready[h % 2], 16)
                    if b == 15:
                        act.wait_ge(acc_free, 1 + L * TILES + (A_GROUPS + 15))
                        act.dma_start(sc[:, 3, :].rearrange("p (g n) -> p g n", g=4),
                                      pool_w[bass.ds(L, 1), :, :, :].rearrange("a p g n -> (a p) g n")).then_inc(pool_w_ready, 16)
                    for n in range(4 * b, 4 * b + 4):
                        for e in SIDE[n]:
                            if e[0] == "cmp_scores":
                                act.wait_ge(v_made, v_count(L, e))
                                nc.scalar.activation(cmp_p[:, :, :], cmp_p[:, :, :], ACT.Exp,
                                                     scale=DH ** -0.5).then_inc(a_made, 1)
                            elif e[0] == "scores":
                                u = e[1]
                                act.wait_ge(s_free, 1 + s_use(L, e) + 1)
                                nc.scalar.activation(pr_of(u), pr_of(u), ACT.Exp, bias=nmax[:, u % 2:u % 2 + 1], scale=-1.0,
                                                     accum_out=den[:, u % 4:u % 4 + 1]).then_inc(a_made, 1)
                            elif e[0] == "scale":
                                act.wait_ge(v_made, v_count(L, e))
                                for u in (e[1], e[1] + 1):
                                    nc.scalar.activation(pr_of(u), pr_of(u), ACT.Copy, scale=scl[:, u % 4:u % 4 + 1]).then_inc(a_made, 1)
                            elif e[0] == "ret_gate":
                                act.wait_ge(acc_free, 1 + L * TILES + (A_GROUPS + B_TILES.index(("rg", e[1])) + 2))
                                nc.scalar.activation(rg_t[:, :], rg[:, :], ACT.Tanh, scale=0.5).then_inc(a_made, 1)
                            elif e[0] == "ret_values" and e[2] == QT - 1:
                                act.wait_ge(pv_done, pv_count(L, e))
                                nc.scalar.activation(pT[:, 1, :], o_bank[e[1] % 2][:, :], ACT.Square).then_inc(a_made, 1)
                                nc.scalar.activation(pT[:, 0, :], o_bank[e[1] % 2][:, :], ACT.Copy).then_inc(o_free, 1)
                            elif e[0] == "ret_var":
                                act.wait_ge(s_done, s_use(L, e))
                                act.wait_ge(con_ready, 16)
                                nc.scalar.activation(pT[:, 1, :], s_of(e)[:, :], ACT.Sqrt, bias=C("eps", 1),
                                                     scale=1.0 / RD).then_inc(a_made, 1)

                with act.Fori(0, DC) as j:
                    for k in range(J_GROUPS):
                        ahead(L, J0 + k, j, J_GROUPS)
                        if 1 <= k <= 4:
                            n = k - 1
                            act.wait_ge(acc_free, 1 + L * TILES + j * 8 + (TJ0 + n + 2))
                            act.wait_ge(con_ready, 16)
                            nc.scalar.activation(work[:, n, :], work[:, n, :], ACT.Tanh, scale=0.5,
                                                 bias=half_b[:, bass.ds(j + n * DC, 1)]).then_inc(tanh_ready, 1)

                for j in range(DC):
                    ahead(L, O0 + j)
                    if j:
                        act.wait_ge(acc_free, 1 + L * TILES + (TO0 + j + 1))
                        nc.scalar.activation(work[:, 2 + (j - 1) % 2, :], x[:, j - 1, :], ACT.Square).then_inc(sq_ready, 1)

                def up(i, g, loop=None):
                    for k in range(2):
                        if loop is None:
                            ahead(L, g + k)
                        else:
                            ahead(L, g + k, loop, 2 * 3)
                        if i is None and k == 0:
                            act.wait_ge(acc_free, 1 + L * TILES + (TO0 + DC + 1))
                            nc.scalar.activation(work[:, 2 + (DC - 1) % 2, :], x[:, DC - 1, :], ACT.Square).then_inc(sq_ready, 1)
                        if i is None and k == 0:
                            root("sumsq2", L)
                        if k == 1:
                            act.wait_ge(conv_ready, L * FC + (1 if i is None else i + 1))
                            nc.scalar.activation(work[:, 2, :], work[:, 1, :], ACT.Tanh, scale=0.5).then_inc(silu_ready, 1)

                up(None, U0)
                with act.Fori(0, (FC - 1) // 3) as t:
                    for k in range(3):
                        up(t * 3 + (k + 1), U0 + 2 + 2 * k, t)

                with act.Fori(0, DC // 2) as t:
                    for k in range(2):
                        for m in range(DG):
                            ahead(L, D0 + DG * k + m, t, 2 * DG)
                        act.wait_ge(acc_free, 1 + L * TILES + t * 2 + (TD0 + k + 2))
                        act.wait_ge(con_ready, 16)
                        nc.scalar.activation(work[:, 2 + k, :], x[:, bass.ds(t * 2 + k, 1), :], ACT.Square).then_inc(sq_ready, 1)

            act.wait_ge(s_done, LAYERS * len(S_USES) + 1)
            nc.scalar.activation(rstd[:, :], s_bank[0][:, :], ACT.Sqrt, bias=C("eps", 1),
                                 scale=1.0 / D).then_inc(root_ready, 1)

        @block.vector
        def _(dve):
            ve = nc.vector
            made = {"s": 0, "t": 0, "v": 0}

            class Chain:

                def __init__(self, s):
                    self.s, self.base, self.n = s, 0, 0

                def __call__(self, ins):
                    self.n += 1
                    ins.then_inc(self.s, 1)
                    dve.wait_ge(self.s, self.base + self.n)

                def turn(self, base, n):
                    self.base, self.n, self.per = base, 0, n

                def end(self):
                    assert self.n == self.per, (self.s, self.n)

            then = Chain(chain)

            def split_x(c, gain, x_c, hi, lo):
                then_ = current[0]
                then_(ve.tensor_scalar(hi, x_c, gain, None, ALU.mult))
                ve.scalar_tensor_tensor(out=lo, in0=x_c, scalar=gain, in1=hi.bitcast(F32),
                                        op0=ALU.mult, op1=ALU.subtract).then_inc(xg_ready, 1)

            current = [then]
            for s in (acc_free, s_free, t_free, o_free):
                dve.sem_inc(s, 2)
            for s in (mrg_ready, act_ready):
                dve.sem_inc(s, 1)
            then(ve.memset(small[:, :], 0.0))
            dve.wait_ge(vec_ready, 16)
            for c in range(DC):
                dve.wait_ge(x_in[c], 16)
                split_x(c, V("norm1", c), x[:, c, :], xg_hi[:, c, :], xg_lo[:, c, :])
            for c in range(DC):
                dve.wait_ge(sq_ready, c + 1)
                if c == 0:
                    ve.tensor_copy(ssq[:, :], first_sq[:, 0, :]).then_inc(ssq_ready, 1)
                else:
                    dve.wait_ge(ssq_ready, c)
                    ve.tensor_tensor(ssq[:, :], ssq[:, :], first_sq[:, c, :], ALU.add).then_inc(ssq_ready, 1)
            CHAIN0 = then.n
            SSQ0 = DC

            with dve.Fori(0, LAYERS) as L:
                then.turn(CHAIN0 + L * CHAIN_LAYER, CHAIN_LAYER)
                current[0] = then

                def take(T, out, in1=None, op=ALU.mult, count=None):
                    dve.wait_ge(halves, 1 + L * (2 * GROUPS) + 2 * (T + 1))
                    ve.tensor_tensor(out, acc[T % 2][0:out.shape[0], :], rstd[0:out.shape[0], :], op).then_inc(acc_free, 1)
                    dve.wait_ge(acc_free, 1 + L * TILES + (T + 2))

                def s_wait(name):
                    dve.wait_ge(s_done, s_use(L, name))

                def s_end(ins, name, wait=False):
                    made["s"] += 1
                    assert S_USES.index(name) + 1 == made["s"], name
                    ins.then_inc(s_free, 1)
                    if wait:
                        dve.wait_ge(s_free, 1 + s_use(L, name) + 1)

                def t_wait(name):
                    dve.wait_ge(t_done, t_use(L, name))

                def t_end(ins, name):
                    made["t"] += 1
                    assert T_USES.index(name) + 1 == made["t"], name
                    ins.then_inc(t_free, 1)

                def v_end(ins, name, wait=False):
                    made["v"] += 1
                    assert V_MADE.index(name) + 1 == made["v"], name
                    ins.then_inc(v_made, 1)
                    if wait:
                        dve.wait_ge(v_made, v_count(L, name))

                def inverse_root(use, n):
                    dve.wait_ge(root_ready, 2 * L + (n + 1))
                    ins = ve.reciprocal(rstd[:, :], rstd[:, :])
                    s_end(ins, use, wait=True)

                def rotate(name, z, cos, sin, parts=(0, 1)):
                    i = ROT[name]
                    r = rot[:, i % 2, :]
                    if 0 in parts:
                        dve.wait_ge(rot_ready[i % 2], rot_value(L, name))
                        ve.tensor_tensor(r, r, C(sin, S), ALU.mult).then_inc(chain, 1)
                        then.n += 1
                        then(ve.tensor_tensor(z, z, C(cos, S), ALU.mult))
                    if 1 in parts:
                        v_end(ve.tensor_tensor(z, z, r, ALU.add), name)

                def rotate_ret(e):
                    kind, h = e[1]
                    rotate(e[1], (rq if kind == "rq" else rk)[:, h % 2, :], "cos_r", "sin_r", (e[2],))

                def windows(src, dst, name):
                    view = src.rearrange("p (m r q) -> p q r m", r=STRIDE // 2, q=2)
                    pe_ = V("pe", 0, BLOCK).rearrange("p (a r q) -> p a q r", a=2, q=2)
                    for g in range(KV_GROUPS):
                        rows = slice(DH * g, DH * g + DH)
                        for q in range(2):
                            for a in range(2):
                                ins = ve.tensor_tensor(
                                    dst[DH * q:DH * q + DH, a * 8:a * 8 + 8, g * NCMP:(g + 1) * NCMP], view[rows, q, :, a:a + NCMP],
                                    pe_[rows, a, q, :].unsqueeze(2).to_broadcast([DH, STRIDE // 2, NCMP]), ALU.add)
                                if (g, q, a) != (1, 1, 1):
                                    ins.then_inc(chain, 1)
                                    then.n += 1
                    v_end(ins, name)

                def gelu_arg(kind):
                    s_wait(f"hid_{kind}")
                    s_end(ve.tensor_copy(hid, s_of(f"hid_{kind}")[0:DH, 0:KV_GROUPS * NCMP]), f"hid_{kind}", wait=True)
                    then(ve.tensor_tensor(hid_a, hid, hid, ALU.mult))
                    then(ve.tensor_scalar(hid_a, hid_a, 0.044715, 1.0, ALU.mult, ALU.add))
                    v_end(ve.tensor_tensor(hid_a, hid_a, hid, ALU.mult), f"arg_{kind}")

                def gelu(kind):
                    dve.wait_ge(a_made, a_count(L, f"hid_{kind}"))
                    v_end(ve.scalar_tensor_tensor(out=hid, in0=hid_a, scalar=1.0, in1=hid,
                                                  op0=ALU.add, op1=ALU.mult), f"hid_{kind}")

                made.update(s=0, t=0, v=0)
                dve.wait_ge(con_ready, 16)
                dve.wait_ge(vec_ready, L * 16 + 16)
                then(ve.tensor_scalar(half_b, V("b_gate", 0, 4 * DC), 0.5, None, ALU.mult))
                then(ve.memset(rot[:, :, :], 0.0))
                for T, tile in enumerate((k_cmp, v_cmp)):
                    dve.wait_ge(halves, 1 + L * (2 * GROUPS) + 2 * (T + 1))
                    ve.tensor_copy(tile[:, :], acc[T][:, :]).then_inc(acc_free, 1)
                    dve.wait_ge(acc_free, 1 + L * TILES + (T + 2))
                inverse_root("sumsq1", 0)
                then(ve.tensor_tensor(k_cmp[:, :], k_cmp[:, :], rstd[:, :], ALU.mult))
                then(ve.tensor_tensor(v_cmp[:, :], v_cmp[:, :], rstd[:, :], ALU.mult))
                windows(k_cmp[:, :], win_k, "win_k")
                take(2, kT[:, 0, :])
                windows(v_cmp[:, :], win_v, "win_v")
                take(3, kT[:, 1, :])
                rotate("k0", kT[:, 0, :], "cos_a", "sin_a")
                take(4, sc[:, 0, :])
                rotate("k1", kT[:, 1, :], "cos_a", "sin_a")
                gelu_arg("k")
                take(5, sc[:, 1, :])
                gelu("k")
                t_wait("v_slc")
                t_end(ve.tensor_copy(v_nat[:, 0, :, :], t_of("v_slc")[:, :].rearrange("p (k n) -> p k n", k=QT)), "v_slc")
                take(6, qT[:, 0, :])
                take(7, qT[:, 1, :])
                t_wait("v_win")
                t_end(ve.tensor_copy(v_nat[:, 1, :, :], t_of("v_win")[:, :].rearrange("p (k n) -> p k n", k=QT)), "v_win")
                rotate("q0", qT[:, 0, :], "cos_a", "sin_a")
                s_wait("kc")
                gelu_arg("v")
                s_end(ve.tensor_scalar(kc[:, 0:NCMP], s_of("kc")[:, 0:NCMP], 0.5, None, ALU.mult), "kc")
                take(8, qT[:, 2, :])
                rotate("q1", qT[:, 1, :], "cos_a", "sin_a")
                gelu("v")
                take(9, qT[:, 3, :])
                rotate("q2", qT[:, 2, :], "cos_a", "sin_a")
                s_wait("vc")
                s_end(ve.tensor_scalar(vc[0:NCMP, :], s_of("vc")[0:NCMP, 0:P], 0.5, None, ALU.mult), "vc")
                s_wait("kc_swap")
                s_end(ve.tensor_tensor(kc_rot[:, 0:NCMP], s_of("kc_swap")[:, 0:NCMP], C("sin_c", NCMP), ALU.mult), "kc_swap", wait=True)
                then(ve.tensor_tensor(kc[:, 0:NCMP], kc[:, 0:NCMP], C("cos_c", NCMP), ALU.mult))
                take(10, sc[:, 2, :])
                rotate("q3", qT[:, 3, :], "cos_a", "sin_a")
                v_end(ve.tensor_tensor(kc[:, 0:NCMP], kc[:, 0:NCMP], kc_rot[:, 0:NCMP], ALU.add), "kc")
                dve.wait_ge(halves, 1 + L * (2 * GROUPS) + 24)
                ve.tensor_copy(pad_out, acc[1][:, 0:2]).then_inc(acc_free, 1)

                def gate(e):
                    s_wait(e)
                    s_end(ve.tensor_scalar(gates[:, :, :], s_of(e)[:, :].rearrange("p (k n) -> p k n", k=QT)[:, :, 0:3 * HEADS],
                                           1.0, 0.5, ALU.add, ALU.mult), e, wait=True)

                def gate_over_sum(qi, branch, sums):
                    then(ve.reciprocal(scale8, sums))
                    g3 = gates[:, qi, :].rearrange("p (h b) -> p b h", b=3)[:, branch, :]
                    then(ve.tensor_tensor(scale8, scale8, g3, ALU.mult))

                def cmp_scores(e):
                    qi = e[1]
                    s_wait(e)
                    src = s_of(e)[:, 0:HEADS * 32].rearrange("p (h n) -> p h n", h=HEADS)[:, :, 0:NCMP]
                    m = C("cmp_mask", QT * NCMP).rearrange("p (q n) -> p q n", q=QT)[:, qi, :]
                    s_end(ve.tensor_tensor(cmp_p[:, :, :], src, m.unsqueeze(1).to_broadcast([P, HEADS, NCMP]), ALU.add), e, wait=True)
                    then(ve.tensor_reduce(c_max, cmp_p[:, :, :], AX.X, ALU.max))
                    v_end(ve.tensor_tensor(cmp_p[:, :, :], cmp_p[:, :, :], c_max.unsqueeze(2).to_broadcast([P, HEADS, NCMP]),
                                           ALU.subtract), e)

                def cmp_scale(e):
                    qi = e[1]
                    dve.wait_ge(a_made, a_count(L, ("cmp_scores", qi)))
                    then(ve.tensor_reduce(c_den, cmp_p[:, :, :], AX.X, ALU.add))
                    gate_over_sum(qi, 0, c_den)
                    if qi == 0:
                        then(ve.tensor_scalar(scale8, scale8, C("seen", 1), None, ALU.mult))
                    v_end(ve.tensor_tensor(cmp_p[:, :, :], cmp_p[:, :, :], scale8.unsqueeze(2).to_broadcast([P, HEADS, NCMP]),
                                           ALU.mult), e)

                def scores(e):
                    u = e[1]
                    w = (unit(u)[0] + 1) * P
                    s_wait(e)
                    alone(dve)
                    s_end(ve.tensor_tensor_reduce(pr_of(u), s_of(e)[:, 0:w], C("causal", S)[:, S - w:S],
                                                  -(DH ** -0.5), 3e38, ALU.add, ALU.min, nmax[:, u % 2:u % 2 + 1]), e)

                def scale(e):
                    u = e[1]
                    qi, br, j = unit(u)
                    sums, out_ = den[:, u % 4:u % 4 + 2], scl[:, u % 4:u % 4 + 2]
                    dve.wait_ge(a_made, a_count(L, ("scores", u + 1)))
                    then(ve.reciprocal(out_, sums))
                    g2 = gates[:, qi, :].rearrange("p (g h b) -> p b h g", g=2, b=3)[:, 1 + br, j, :]
                    v_end(ve.tensor_tensor(out_, out_, g2, ALU.mult), e)

                def turn(e):
                    u = e[1]
                    w = (unit(u)[0] + 1) * P
                    t_wait(e)
                    if u >= 2:
                        dve.wait_ge(pv_done, pv_count(L, ("values", u - 2)))
                    t_end(ve.tensor_copy(pT[:, u % 2, 0:w], t_of(e)[:, 0:w]), e)

                def values(e):
                    u = e[1]
                    if u % 16 != 14:
                        return
                    qi = unit(u)[0]
                    dve.wait_ge(pv_done, pv_count(L, ("values", u + 1)))
                    src = o_bank[qi % 2][:, :].rearrange("p (j n) -> p j n", j=BC)
                    hi, lo = (y[1][:, :, qi * P:(qi + 1) * P] for y in (y_hi, y_lo))
                    then(ve.tensor_copy(hi, src))
                    ve.tensor_tensor(lo, src, hi.bitcast(F32), ALU.subtract).then_inc(o_free, 1)

                def cmp_turn(e):
                    for half in range(2):
                        t_wait((*e, half))
                        if e[1]:
                            dve.wait_ge(pv_done, pv_count(L, ("values", 16 * e[1] - 1)))
                        t_end(ve.tensor_copy(cmp_pT[0:NCMP, half, :], t_of((*e, half))[0:NCMP, :]), (*e, half))

                def ret_scores(e):
                    h, m = e[1], e[2]
                    w = S - m * P
                    s_wait(e)
                    if m == 0:
                        dve.wait_ge(dec_ready[h % 2], L * 32 + 16 * (h // 2 + 1))
                    r = QT * h + m
                    if r >= 2:
                        dve.wait_ge(pv_done, pv_count(L, ("ret_values", (r - 2) // QT, (r - 2) % QT)))
                    s_end(ve.tensor_tensor(pr[:, m % 2, 0:w], s_of(e)[:, 0:w], dec[:, h % 2, 0:w], ALU.mult), e)

                def ret_turn(e):
                    t_wait(e)
                    src = t_of(e)[:, :].rearrange("p (k n) -> p k n", k=QT)
                    then(ve.tensor_reduce(v_sum, src, AX.X, ALU.add))
                    t_end(ve.scalar_tensor_tensor(out=rv[:, :, :], in0=v_sum.unsqueeze(2).to_broadcast([P, QT, RD]),
                                                  scalar=-1.0 / RD, in1=src, op0=ALU.mult, op1=ALU.add), e)

                def ret_gate(e):
                    dve.wait_ge(a_made, a_count(L, e))
                    then(ve.scalar_tensor_tensor(out=rg[:, :], in0=rg_t[:, :], scalar=1.0, in1=rg[:, :],
                                                 op0=ALU.add, op1=ALU.mult))

                def ret_var(e):
                    dve.wait_ge(a_made, a_count(L, e))
                    then(ve.reciprocal(pT[:, 1, 0:S // 2], pT[:, 1, 0:S // 2]))

                def ret_inverse(e):
                    s_end(ve.reciprocal(pT[:, 1, S // 2:S], pT[:, 1, S // 2:S]), ("ret_var", e[1]), wait=True)

                def split_y(n, j, src):
                    hi, lo = y_hi[n][:, j, :], y_lo[n][:, j, :]
                    then(ve.tensor_copy(hi, src))
                    then(ve.tensor_tensor(lo, src, hi.bitcast(F32), ALU.subtract))

                def ret_end(e):
                    h = e[1]
                    o = pT[:, 0, :]
                    dve.wait_ge(o_free, 1 + L * OUTS + (QT + h + 2))
                    then(ve.scalar_tensor_tensor(out=o, in0=o, scalar=V("ret_gn", h), in1=pT[:, 1, :],
                                                 op0=ALU.mult, op1=ALU.mult))
                    then(ve.scalar_tensor_tensor(out=o, in0=o, scalar=0.5, in1=rg[:, :], op0=ALU.mult, op1=ALU.mult))

                def ret_split(e):
                    split_y(2, e[1], pT[:, 0, :])

                def pool(e):
                    g = e[1]
                    s_wait(e)
                    sc_ = V("pool_scale", g)
                    hi, lo = y_hi[3][:, g, :], y_lo[3][:, g, :]
                    then(ve.tensor_scalar(hi, s_of(e)[:, :], sc_, None, ALU.mult))
                    s_end(ve.scalar_tensor_tensor(out=lo, in0=s_of(e)[:, :], scalar=sc_, in1=hi.bitcast(F32),
                                                  op0=ALU.mult, op1=ALU.subtract), e)

                def conv(e):
                    j, part = e[1], e[2]
                    t, y, b = sc[:, 1, :], sc[:, 2, :], sc[:, 3, :]
                    tap = lambda k: V("sc_conv", 3 * j + k)
                    hi, lo = y_hi[0][:, j, :], y_lo[0][:, j, :]
                    if part == 0:
                        then(ve.tensor_scalar(y, t, tap(2), None, ALU.mult))
                        then(ve.scalar_tensor_tensor(out=y[:, 1:S], in0=t[:, 0:S - 1], scalar=tap(1), in1=y[:, 1:S], op0=ALU.mult, op1=ALU.add))
                    elif part == 1:
                        then(ve.scalar_tensor_tensor(out=y[:, 2:S], in0=t[:, 0:S - 2], scalar=tap(0), in1=y[:, 2:S], op0=ALU.mult, op1=ALU.add))
                        then(ve.tensor_tensor(y, y, b, ALU.mult))
                    elif part == 2:
                        then(ve.tensor_copy(hi, y))
                    else:
                        then(ve.tensor_tensor(lo, y, hi.bitcast(F32), ALU.subtract))

                def mean(e):
                    g, part = e[1], e[2]
                    u, n = sc[:, 0, :], POOLS[g]
                    buf = lambda k: u if k == 0 else sc[:, 1 + k % 2, :]
                    if part <= g:
                        src, dst, k = buf(part), buf(part + 1), 1 << part
                        then(ve.tensor_copy(dst[:, 0:k], src[:, 0:k]))
                        then(ve.tensor_tensor(dst[:, k:S], src[:, k:S], src[:, 0:S - k], ALU.add))
                    if part == 3:
                        src = buf(g + 1)
                        fix = C("pool_fix", 64)[:, 16 * g:16 * g + n - 1]
                        then(ve.tensor_tensor(src[:, 0:n - 1], src[:, 0:n - 1], fix, ALU.mult))
                        v_end(ve.scalar_tensor_tensor(out=pooled[g], in0=src, scalar=1.0 / n, in1=u, op0=ALU.mult, op1=ALU.subtract),
                              ("u", g), wait=True)

                steps = {"gate": gate, "cmp_scores": cmp_scores, "scores": scores, "turn": turn, "values": values,
                         "cmp_turn": cmp_turn, "cmp_scale": cmp_scale, "scale": scale, "ret_scores": ret_scores,
                         "ret_turn": ret_turn, "ret_gate": ret_gate, "ret_var": ret_var,
                         "ret_inverse": ret_inverse, "ret_end": ret_end, "ret_split": ret_split, "pool": pool, "conv": conv, "mean": mean, "rotate": rotate_ret}

                for b in range(B_GROUPS):
                    for n in range(4 * b, 4 * b + 4):
                        for e in SIDE[n]:
                            if e[0] in steps:
                                steps[e[0]](e)
                    kind, i = B_TILES[b]
                    T = A_GROUPS + b
                    take(T, {"rq": rq[:, i % 2, :], "rk": rk[:, i % 2, :], "rv": rv_T[:, :], "rg": rg[:, :], "c": sc[:, 0, :],
                             "h": sc[:, 1, :], "b": sc[:, 3, :], "u": sc[:, 0, :]}[kind])
                    if kind == "h":
                        then(ve.tensor_tensor(sc[:, 1, :], sc[:, 1, :], sc[:, 0, :], ALU.mult))
                for k in range(4):
                    conv(("conv", B_TILES[-1][1], k))
                v_end(ve.memset(ssq[:, :], 0.0), "branches")

                with dve.Fori(0, DC) as j:
                    cj = Chain(chain_j)
                    cj.turn(L * (DC * CHAIN_J) + j * CHAIN_J, CHAIN_J)
                    dve.wait_ge(mrg_ready, 1 + L * DC + j)
                    for n in range(4):
                        dve.wait_ge(halves, 1 + L * (2 * GROUPS) + j * (2 * J_GROUPS) + (2 * J0 + 2 * (n + 1)))
                        ve.tensor_tensor(work[:, n, :], acc[n % 2][:, :], rstd[:, :], ALU.mult).then_inc(acc_free, 1)
                        dve.wait_ge(acc_free, 1 + L * TILES + j * 8 + (TJ0 + n + 2))
                    for n in range(4):
                        dve.wait_ge(tanh_ready, L * (4 * DC) + j * 4 + (n + 1))
                        dve.wait_ge(halves, 1 + L * (2 * GROUPS) + j * (2 * J_GROUPS) + (2 * J0 + 8 + (n + 1)))
                        ve.scalar_tensor_tensor(out=work[:, n, :], in0=work[:, n, :], scalar=1.0, in1=acc[n % 2][:, :],
                                                op0=ALU.add, op1=ALU.mult).then_inc(acc_free, 1)
                        dve.wait_ge(acc_free, 1 + L * TILES + j * 8 + (TJ0 + 4 + n + 2))
                        if n:
                            cj(ve.tensor_tensor(work[:, 0, :], work[:, 0, :], work[:, n, :], ALU.add))
                    hi, lo = mrg_hi[:, bass.ds(j, 1), :], mrg_lo[:, bass.ds(j, 1), :]
                    src = work[:, 0:1, :]
                    alone(dve)
                    cj(ve.tensor_copy(hi, src))
                    ve.tensor_tensor(lo, src, hi.bitcast(F32), ALU.subtract).then_inc(mrg_ready, 1)
                    cj.end()

                def add_square(buf, value, c):
                    dve.wait_ge(sq_ready, value)
                    dve.wait_ge(ssq_ready, value - 1)
                    ve.tensor_tensor(ssq[:, :], ssq[:, :], work[:, buf, :], ALU.add).then_inc(ssq_ready, 1)

                dve.wait_ge(v_made, v_count(L, "branches"))
                for j in range(DC):
                    T = TO0 + j
                    dve.wait_ge(halves, 1 + L * (2 * GROUPS) + 2 * (O0 + j + 1))
                    ve.scalar_tensor_tensor(out=x[:, j, :], in0=acc[T % 2][:, :], scalar=0.5, in1=x[:, j, :],
                                            op0=ALU.mult, op1=ALU.add).then_inc(acc_free, 1)
                    dve.wait_ge(acc_free, 1 + L * TILES + (T + 2))
                    split_x(j, V("norm2", j), x[:, j, :], xg_hi[:, j, :], xg_lo[:, j, :])
                    if j:
                        add_square(2 + (j - 1) % 2, L * 16 + (SSQ0 + j), j)
                add_square(2 + (DC - 1) % 2, L * 16 + (SSQ0 + DC), DC)

                def up(i, T_gate, cf, halves_gate, acc_gate):
                    u, c, t, v = (work[:, k, :] for k in range(4))
                    tap = lambda k: (V("ffn_conv", 3 * i + k) if isinstance(i, int)
                                     else vc_[:, bass.ds(i * 3 + (VEC["ffn_conv"] + k), 1)])
                    dve.wait_ge(act_ready, 1 + L * FC + i)
                    dve.wait_ge(halves, 1 + halves_gate)
                    ve.tensor_tensor(u, acc[0][:, :], rstd[:, :], ALU.mult).then_inc(acc_free, 1)
                    dve.wait_ge(acc_free, 1 + acc_gate)
                    cf(ve.tensor_scalar(c, u, tap(2), None, ALU.mult))
                    cf(ve.scalar_tensor_tensor(out=c[:, 1:S], in0=u[:, 0:S - 1], scalar=tap(1), in1=c[:, 1:S], op0=ALU.mult, op1=ALU.add))
                    ve.scalar_tensor_tensor(out=c[:, 2:S], in0=u[:, 0:S - 2], scalar=tap(0), in1=c[:, 2:S],
                                            op0=ALU.mult, op1=ALU.add).then_inc(conv_ready, 1)
                    dve.wait_ge(silu_ready, L * FC + (i + 1))
                    cf(ve.scalar_tensor_tensor(out=t, in0=t, scalar=1.0, in1=c, op0=ALU.add, op1=ALU.mult))
                    dve.wait_ge(halves, 1 + halves_gate + 2)
                    ve.tensor_tensor(v, acc[1][:, :], rstd[:, :], ALU.mult).then_inc(acc_free, 1)
                    dve.wait_ge(acc_free, 1 + acc_gate + 1)
                    cf(ve.tensor_tensor(t, t, v, ALU.mult))
                    if isinstance(i, int):
                        hi, lo, t3 = act_hi[:, i, :], act_lo[:, i, :], t
                    else:
                        hi, lo, t3 = act_hi[:, bass.ds(i, 1), :], act_lo[:, bass.ds(i, 1), :], work[:, 2:3, :]
                    alone(dve)
                    cf(ve.tensor_copy(hi, t3))
                    ve.tensor_tensor(lo, t3, hi.bitcast(F32), ALU.subtract).then_inc(act_ready, 1)

                inverse_root("sumsq2", 1)
                assert made == {"s": len(S_USES), "t": len(T_USES), "v": len(V_MADE)}
                up(0, TU0, then, L * (2 * GROUPS) + 2 * (U0 + 1), L * TILES + (TU0 + 2))
                then.end()
                alone(dve)
                with dve.Fori(0, (FC - 1) // 3) as t:
                    cf = Chain(chain_f)
                    cf.turn((L * ((FC - 1) // 3) + t) * CHAIN_F, CHAIN_F)
                    for k in range(3):
                        i = t * 3 + (k + 1)
                        up(i, None, cf, L * (2 * GROUPS) + t * 12 + (2 * U0 + 4 * (k + 1) + 2),
                           L * TILES + t * 6 + (TU0 + 2 * (k + 1) + 2))
                    cf.end()

                dve.wait_ge(vec_ready, L * 16 + 32)
                dve.wait_ge(act_ready, 1 + L * FC + FC)
                ve.memset(ssq[:, :], 0.0).then_inc(ssq_zero, 1)
                dve.wait_ge(ssq_zero, L + 1)
                alone(dve)
                with dve.Fori(0, DC // 2) as t:
                    cd = Chain(chain_d)
                    cd.turn((L * (DC // 2) + t) * CHAIN_D, CHAIN_D)
                    current[0] = cd
                    for k in range(2):
                        c = t * 2 + k
                        x_c = x[:, bass.ds(c, 1), :]
                        a3 = acc[k][:, :].unsqueeze(1)
                        dve.wait_ge(halves, 1 + L * (2 * GROUPS) + t * (4 * DG) + (2 * D0 + 2 * DG * (k + 1)))
                        ve.scalar_tensor_tensor(out=x_c, in0=a3, scalar=0.5, in1=x_c,
                                                op0=ALU.mult, op1=ALU.add).then_inc(acc_free, 1)
                        dve.wait_ge(acc_free, 1 + L * TILES + t * 2 + (TD0 + k + 2))
                        split_x(c, vc_[:, bass.ds(c + VEC["norm1"], 1)], x_c,
                                xg_hi[:, bass.ds(c, 1), :], xg_lo[:, bass.ds(c, 1), :])
                        add_square(2 + k, L * 16 + t * 2 + (SSQ0 + DC + k + 1), None)
                    cd.end()

            dve.wait_ge(root_ready, 2 * LAYERS + 1)
            ve.reciprocal(rstd[:, :], rstd[:, :]).then_inc(s_free, 1)
            dve.wait_ge(s_free, 1 + LAYERS * len(S_USES) + 2)
            for c in range(DC):
                ve.scalar_tensor_tensor(out=x[:, c, :], in0=x[:, c, :], scalar=V("norm1", c), in1=rstd[:, :],
                                        op0=ALU.mult, op1=ALU.mult).then_inc(y_ready, 1)

        @block.tensor
        def _(pe):
            mm = nc.tensor.matmul
            used = {"s": 0, "t": 0}
            pe.sem_inc(halves, 1)

            def product(tile, slot, chunk, right_hi, right_lo, first, last):
                w_h, w_l = (w[:, slot, chunk * P:(chunk + 1) * P] for w in (w_hi, w_lo))
                mm(tile, w_h, right_hi, start=first, stop=False)
                mm(tile, w_h, right_lo, start=False, stop=False)
                return mm(tile, w_l, right_hi, start=False, stop=last)

            with pe.Fori(0, LAYERS) as L:
                used.update(s=0, t=0)

                def group_here(g, loop=None, per=0):
                    v = L * GROUPS + (g + 1)
                    if loop is not None:
                        v = v + loop * per
                    pe.wait_ge(hi_ready, v)
                    pe.wait_ge(lo_ready, 1 + v)

                def tile_free(T, loop=None, per=0):
                    v = L * TILES + T
                    if loop is not None:
                        v = v + loop * per
                    pe.wait_ge(acc_free, 1 + v)

                def quarter(g, q, tile, wait=False):
                    for c in (2 * q, 2 * q + 1):
                        if wait:
                            pe.wait_ge(xg_ready, L * 16 + (c + 1 + wait - 1))
                        ins = product(tile[:, :], g % RING, c, xg_hi[:, c, :], xg_lo[:, c, :], c == 0, c == CH - 1)
                    if q % 2:
                        ins.then_inc(halves, 1)

                def projection(g, tile, wait=False, norm=None):
                    for q in range(4):
                        quarter(g, q, tile, wait)
                        if norm and q == 2:
                            sum_squares(*norm)

                def s_begin(name):
                    used["s"] += 1
                    assert S_USES.index(name) + 1 == used["s"], name
                    pe.wait_ge(s_free, 1 + L * len(S_USES) + S_USES.index(name))
                    return s_of(name)

                def t_begin(name):
                    used["t"] += 1
                    assert T_USES.index(name) + 1 == used["t"], name
                    pe.wait_ge(t_free, 1 + L * len(T_USES) + T_USES.index(name))
                    return t_of(name)

                def last_wait():
                    pe.wait_ge(con_ready, 16)

                def sum_squares(use, value):
                    pe.wait_ge(ssq_ready, value)
                    b = s_begin(use)
                    last_wait()
                    mm(b[:, :], ones, ssq[:, :], start=True, stop=True).then_inc(s_done, 1)

                def compress(kind, w1_, win, i):
                    pe.wait_ge(v_made, v_count(L, f"win_{kind}"))
                    pe.wait_ge(w1_ready[i], L * 16 + 16)
                    b = s_begin(f"hid_{kind}")
                    last_wait()
                    for l in range(BLOCK // 2):
                        ins = mm(b[0:DH, 0:KV_GROUPS * NCMP], w1_[:, l, :], win[:, l, :], start=(l == 0), stop=(l == BLOCK // 2 - 1))
                    ins.then_inc(s_done, 1)

                def turn4(name, src):
                    b = t_begin(name)
                    last_wait()
                    for k in range(QT):
                        ins = nc.tensor.transpose(b[:, k * P:(k + 1) * P], src[:, k * P:(k + 1) * P], ident)
                    ins.then_inc(t_done, 1)

                for g, name in enumerate(A_TILES):
                    group_here(g)
                    tile_free(g)
                    if name == "pad":
                        for _ in range(2):
                            mm(acc[1][:, 0:2], w_hi[:, g % RING, 0:P], xg_hi[:, 0, 0:2], start=True, stop=True).then_inc(halves, 1)
                    else:
                        projection(g, acc[g % 2], wait=1 if g == 0 else False)
                    if g == 1:
                        sum_squares("sumsq1", L * 16 + DC)
                    if g == 4:
                        compress("k", w1k, win_k, 0)
                    if g == 6:
                        compress("v", w1v, win_v, 1)
                    if g == 7:
                        pe.wait_ge(v_made, v_count(L, "hid_k"))
                        b = s_begin("kc")
                        alone(pe)
                        for i in range(KV_GROUPS):
                            ins = mm(b[DH * i:DH * i + DH, 0:NCMP], V("w2k", 0, DH)[0:DH, :], hid[:, i * NCMP:(i + 1) * NCMP],
                                     start=True, stop=True)
                        ins.then_inc(s_done, 1)
                    if g == 9:
                        pe.wait_ge(v_made, v_count(L, "hid_v"))
                        b = s_begin("vc")
                        alone(pe)
                        for i in range(KV_GROUPS):
                            ins = mm(b[0:NCMP, DH * i:DH * i + DH], hid[:, i * NCMP:(i + 1) * NCMP], V("w2v", 0, DH)[0:DH, :],
                                     start=True, stop=True)
                        ins.then_inc(s_done, 1)
                        b = s_begin("kc_swap")
                        pe.wait_ge(s_free, 1 + s_use(L, "kc") + 1)
                        last_wait()
                        mm(b[:, 0:NCMP], swap, kc[:, 0:NCMP], start=True, stop=True).then_inc(s_done, 1)
                    if g in (5, 7):
                        i = (g - 5) // 2
                        pe.wait_ge(acc_free, 1 + L * TILES + (4 + i + 2))
                        turn4(("v_slc", "v_win")[i], sc[:, i, :])

                def gate(e):
                    pe.wait_ge(a_made, a_count(L, "gate"))
                    b = s_begin(e)
                    alone(pe)
                    for k in range(QT):
                        ins = nc.tensor.transpose(b[:, k * P:k * P + 32], sc[0:32, 2, k * P:(k + 1) * P], ident[0:32, 0:32])
                    ins.then_inc(s_done, 1)

                def cmp_scores(e):
                    qi = e[1]
                    if qi == 0:
                        pe.wait_ge(v_made, v_count(L, "kc"))
                    b = s_begin(e)
                    last_wait()
                    for h in range(HEADS):
                        r = slice(64 * (h // 4), 64 * (h // 4) + 64)
                        ins = mm(b[:, 32 * h:32 * h + NCMP], qT[r, h % 4, qi * P:(qi + 1) * P], kc[r, 0:NCMP], start=True, stop=True)
                        if h == 3:
                            ins.then_inc(rows_done, 1)
                            pe.wait_ge(rows_done, L * QT + (qi + 1))
                    ins.then_inc(s_done, 1)

                def scores(e):
                    qi, br, h = unit(e[1])
                    w = (qi + 1) * P
                    r = slice(64 * (h // 4), 64 * (h // 4) + 64)
                    b = s_begin(e)
                    last_wait()
                    mm(b[:, 0:w], qT[r, h % 4, qi * P:(qi + 1) * P], kT[r, br, 0:w], start=True, stop=True).then_inc(s_done, 1)

                def turn(e):
                    u = e[1]
                    pe.wait_ge(a_made, a_count(L, ("scale", u)))
                    b = t_begin(e)
                    last_wait()
                    for k in range(unit(u)[0] + 1):
                        ins = nc.tensor.transpose(b[:, k * P:(k + 1) * P], pr_of(u)[:, k * P:(k + 1) * P], ident)
                    ins.then_inc(t_done, 1)

                def values(e):
                    u = e[1]
                    qi, br, j = unit(u)
                    pe.wait_ge(t_free, 1 + t_use(L, ("turn", u + 1)) + 1)
                    if u % 16 == 0:
                        pe.wait_ge(o_free, 1 + L * OUTS + qi)
                    last_wait()
                    products = [(v_nat[:, br, k, :], pT[:, :, k * P:(k + 1) * P]) for k in range(qi + 1)]
                    if br == 1:
                        products.append((vc[0:NCMP, :], cmp_pT[0:NCMP, :, j * P:(j + 1) * P]))
                    for k, (v, p) in enumerate(products):
                        for half in range(2):
                            d = slice(DH * half, DH * half + DH)
                            ins = mm(o_bank[qi % 2][d, j * P:(j + 1) * P], v[:, d], p[:, half, :],
                                     start=(br == 0 and k == 0), stop=(br == 1 and k == qi + 1))
                            if k == len(products) - 1:
                                ins.then_inc(pv_done, 1)

                def cmp_turn(e):
                    pe.wait_ge(v_made, v_count(L, ("cmp_scale", e[1])))
                    for half in range(2):
                        b = t_begin((*e, half))
                        last_wait()
                        for i in range(4):
                            ins = nc.tensor.transpose(b[0:NCMP, i * P:(i + 1) * P], cmp_p[:, 4 * half + i, :], ident)
                        ins.then_inc(t_done, 1)

                def ret_turn(e):
                    pe.wait_ge(acc_free, 1 + L * TILES + (A_GROUPS + B_TILES.index(("rv", e[1])) + 2))
                    turn4(e, rv_T[:, :])

                def ret_scores(e):
                    h, m = e[1], e[2]
                    if m == 0:
                        pe.wait_ge(v_made, v_count(L, ("rk", h)))
                    b = s_begin(e)
                    last_wait()
                    mm(b[:, 0:S - m * P], rk[:, h % 2, m * P:(m + 1) * P], rq[:, h % 2, m * P:S],
                       start=True, stop=True).then_inc(s_done, 1)

                def ret_values(e):
                    h, m = e[1], e[2]
                    pe.wait_ge(s_free, 1 + s_use(L, ("ret_scores", h, m)) + 1)
                    if m == 0:
                        pe.wait_ge(t_free, 1 + t_use(L, ("ret_turn", h)) + 1)
                        pe.wait_ge(o_free, 1 + L * OUTS + (QT + h))
                    last_wait()
                    mm(o_bank[h % 2][:, m * P:S], rv[:, m, :], pr[:, m % 2, 0:S - m * P],
                       start=(m == 0), stop=(m == QT - 1)).then_inc(pv_done, 1)

                def ret_var(e):
                    pe.wait_ge(a_made, a_count(L, ("ret_values", e[1], QT - 1)))
                    b = s_begin(e)
                    last_wait()
                    mm(b[:, :], ones, pT[:, 1, :], start=True, stop=True).then_inc(s_done, 1)

                def pool(e):
                    g = e[1]
                    if g == 1:
                        pe.wait_ge(pool_w_ready, L * 16 + 16)
                    pe.wait_ge(v_made, v_count(L, ("u", g)))
                    b = s_begin(e)
                    last_wait()
                    mm(b[:, :], sc[:, 3, g * P:(g + 1) * P], pooled[g], start=True, stop=True).then_inc(s_done, 1)

                steps = {"gate": gate, "cmp_scores": cmp_scores, "scores": scores, "turn": turn, "values": values,
                         "cmp_turn": cmp_turn, "ret_scores": ret_scores, "ret_values": ret_values,
                         "ret_turn": ret_turn, "ret_var": ret_var, "pool": pool}

                for b in range(B_GROUPS):
                    g = A_GROUPS + b
                    group_here(g)
                    tile_free(g)
                    for q in range(4):
                        quarter(g, q, acc[g % 2])
                        for e in SIDE[4 * b + q]:
                            if e[0] in steps:
                                steps[e[0]](e)

                with pe.Fori(0, DC) as j:
                    for n in range(4):
                        group_here(J0 + n, j, J_GROUPS)
                        tile_free(TJ0 + n, j, 8)
                        projection(J0 + n, acc[n % 2])
                    for n in range(4):
                        g = J0 + 4 + n // 2
                        if n % 2 == 0:
                            group_here(g, j, J_GROUPS)
                        tile_free(TJ0 + 4 + n, j, 8)
                        if n == 0:
                            pe.wait_ge(v_made, v_count(L, "branches"))
                        for c in range(BC):
                            ins = product(acc[n % 2][:, :], g % RING, BC * (n % 2) + c, y_hi[n][:, c, :], y_lo[n][:, c, :],
                                          c == 0, c == BC - 1)
                        ins.then_inc(halves, 1)

                for j in range(DC):
                    g, T = O0 + j, TO0 + j
                    group_here(g)
                    tile_free(T)
                    for c in range(DC):
                        if j == 0:
                            pe.wait_ge(mrg_ready, 1 + L * DC + (c + 1))
                        ins = product(acc[T % 2][:, :], g % RING, c, mrg_hi[:, c, :], mrg_lo[:, c, :], c == 0, c == DC - 1)
                        if c % 4 == 3:
                            ins.then_inc(halves, 1)

                for k in range(2):
                    group_here(U0 + k)
                    tile_free(TU0 + k)
                    projection(U0 + k, acc[k], wait=DC + 1 if k == 0 else False,
                               norm=("sumsq2", L * 16 + 2 * DC) if k == 0 else None)
                assert used == {"s": len(S_USES), "t": len(T_USES)}
                with pe.Fori(0, (FC - 1) // 3) as t:
                    for k in range(6):
                        group_here(U0 + 2 + k, t, 6)
                        tile_free(TU0 + 2 + k, t, 6)
                        projection(U0 + 2 + k, acc[k % 2])

                with pe.Fori(0, DC // 2) as t:
                    for k in range(2):
                        tile_free(TD0 + k, t, 2)
                        for c in range(FC):
                            g = D0 + DG * k + c // CH
                            if c % CH == 0:
                                group_here(g, t, 2 * DG)
                            if c == 0:
                                pe.wait_ge(act_ready, 1 + L * FC + (FC - 1))
                            if c == FC - 1:
                                pe.wait_ge(act_ready, 1 + L * FC + FC)
                            ins = product(acc[k][:, :], g % RING, c % CH, act_hi[:, c, :], act_lo[:, c, :], c == 0, c == FC - 1)
                            if c % 4 == 3 or c == FC - 1:
                                ins.then_inc(halves, 1)

            pe.wait_ge(ssq_ready, LAYERS * 16 + DC)
            pe.wait_ge(s_free, 1 + LAYERS * len(S_USES))
            mm(s_bank[0][:, :], ones, ssq[:, :], start=True, stop=True).then_inc(s_done, 1)


CHAIN_LAYER, CHAIN_J, CHAIN_F, CHAIN_D = 201, 4, 15, 2


def _constants():
    con = np.zeros((P, NCON), np.float32)

    def put(name, a):
        con[0:a.shape[0], CON[name]:CON[name] + a.shape[1]] = a

    put("ident", np.eye(P, dtype=np.float32))
    swap = np.zeros((P, P), np.float32)
    for o in (0, 64):
        for i in range(8):
            swap[o + i, o + 8 + i] = swap[o + 8 + i, o + i] = 1
    put("swap", swap)
    put("ones", np.ones((P, P), np.float32))
    p, f = np.arange(P)[:, None], np.arange(S)[None, :]
    put("causal", np.where(f - (S - P) > p, NEG, 0).astype(np.float32))
    ends = np.arange(NCMP) * STRIDE + BLOCK - 1
    for qi in range(QT):
        m = np.where(ends[None, :] <= qi * P + p, 0, NEG).astype(np.float32)
        con[:, CON["cmp_mask"] + qi * NCMP:CON["cmp_mask"] + (qi + 1) * NCMP] = m
    put("seen", (p >= BLOCK - 1).astype(np.float32))
    con[:, CON["eps"]] = EPS

    def angles(theta, half, pos):
        inv = np.power(np.float32(theta), -np.arange(half, dtype=np.float32) / np.float32(half))
        a = (pos.astype(np.float32)[None, :] * inv[:, None]).astype(np.float32)
        return np.cos(a).astype(np.float32), np.sin(a).astype(np.float32)

    for suffix, pos in (("a", np.arange(S)), ("c", ends)):
        c, s = angles(500000.0, 8, pos)
        cos, sin = np.ones((P, len(pos)), np.float32), np.zeros((P, len(pos)), np.float32)
        for o in (0, 64):
            cos[o:o + 8], cos[o + 8:o + 16] = c, c
            sin[o:o + 8], sin[o + 8:o + 16] = -s, s
        put(f"cos_{suffix}", cos)
        put(f"sin_{suffix}", sin)
    c, s = angles(10000.0, RD // 2, np.arange(S))
    put("cos_r", np.concatenate([c, c]))
    put("sin_r", np.concatenate([-s, s]))
    for g, n in enumerate(POOLS):
        con[:, CON["pool_fix"] + 16 * g:CON["pool_fix"] + 16 * g + n - 1] = n / np.arange(1, n, dtype=np.float32)
    log_g = np.log1p(-np.exp2(-5.0 - np.arange(RH)))
    diff = (f - p)[None]
    dec = np.where(diff >= 0, np.exp(np.maximum(diff, 0) * log_g[:, None, None]), 0) * RD ** -0.5
    return con, dec.astype(np.float32)


def _tiles(w):
    k, m = w.shape
    return w.reshape(k // P, P, m // P, P).transpose(2, 1, 0, 3)


def _weights(w_in, w_branch, w_o, w_up, w_down):
    at = np.cumsum([0, 3 * BW, HEADS * DH, 3 * 2 * KV_GROUPS * DH, 3 * HEADS, 4 * BW, BW])
    z_sc, z_q, z_kv, z_ng, z_ret, z_pool, z_gate = (w_in[:, a:b] for a, b in zip(at, [*at[1:], w_in.shape[1]]))
    kv = _tiles(z_kv)
    q = z_q.reshape(D, 2, 4, DH).transpose(0, 2, 1, 3).reshape(D, HEADS * DH)
    ng = np.zeros((D, P), np.float32)
    ng[:, 0:3 * HEADS] = z_ng
    a = [kv[0], kv[1], kv[2], kv[4], kv[3], kv[5], *_tiles(q), _tiles(ng)[0], np.zeros((P, CH, P), np.float32)]
    ret, sc, pool = _tiles(z_ret), _tiles(z_sc), _tiles(z_pool)
    part = {"rq": (ret, 0), "rk": (ret, 4), "rv": (ret, 8), "rg": (ret, 12), "b": (sc, 0), "c": (sc, 4), "h": (sc, 8), "u": (pool, 0)}
    b = [part[k][0][part[k][1] + i] for k, i in B_TILES]
    w_attn = w_branch[1].reshape(2, 4, DH, D).transpose(1, 0, 2, 3).reshape(BW, D)
    gate, branch = _tiles(z_gate), [_tiles(w) for w in (w_branch[0], w_attn, w_branch[2], w_branch[3])]
    js = []
    for j in range(DC):
        js += [gate[n * DC + j] for n in range(4)]
        js += [np.concatenate([branch[n][j], branch[n + 1][j]], axis=1) for n in (0, 2)]
    up = _tiles(w_up)
    ups = [up[k * FC + i] for i in range(FC) for k in range(2)]
    down = np.zeros((DC, P, DG * CH, P), np.float32)
    down[:, :, 0:FC] = _tiles(w_down)
    downs = [down[j, :, CH * m:CH * (m + 1)] for j in range(DC) for m in range(DG)]
    return np.stack([*a, *b, *js, *_tiles(w_o), *ups, *downs]).reshape(GROUPS, P, CH * P)


def kernel(**inputs):
    import concourse.bacc as bacc
    from concourse.bass_utils import run_bass_kernel_spmd

    i = {k: np.asarray(v) for k, v in inputs.items()}
    arrays = {"xT": np.ascontiguousarray(i["x"][0].T.reshape(DC, P, S).transpose(1, 0, 2))}
    groups = [_weights(*(i[k][l] for k in ("w_in", "w_branch", "w_o", "w_up", "w_down"))) for l in range(LAYERS)]
    arrays["weights"] = np.concatenate([*groups, np.zeros((RING, P, CH * P), np.float32)])

    def cols(a, n):
        return a.reshape(-1, n, P).transpose(2, 1, 0).reshape(P, -1)

    def pairs(w):
        return w.reshape(BLOCK // 2, 2, DH, DH).transpose(1, 2, 0, 3).reshape(P, BLOCK // 2, DH)

    vec = np.zeros((LAYERS + 1, P, NVEC), np.float32)
    for l in range(LAYERS):
        parts = {"norm1": cols(i["norm1_g"][l], DC), "norm2": cols(i["norm2_g"][l], DC), "b_gate": cols(i["b_gate"][l], 4 * DC),
                 "sc_conv": cols(i["sc_conv"][l], BC), "ret_gn": cols(i["ret_gn_g"][l], BC),
                 "pool_scale": cols(i["pool_scale"][l], BC), "ffn_conv": cols(i["ffn_conv"][l], FC),
                 "pe": np.concatenate([i["cmp_pe"][l].T] * KV_GROUPS), "w2k": i["cmp_w2_k"][l], "w2v": i["cmp_w2_v"][l]}
        for name, a in parts.items():
            vec[l, 0:a.shape[0], VEC[name]:VEC[name] + a.shape[1]] = a
    vec[LAYERS, :, 0:DC] = cols(i["final_norm_g"], DC)
    arrays["vec"] = vec
    arrays["w1"] = np.stack([pairs(i[k][l]) for l in range(LAYERS) for k in ("cmp_w1_k", "cmp_w1_v")])
    arrays["pool_w"] = np.ascontiguousarray(i["pool_w"].transpose(0, 2, 1, 3))
    arrays["consts"], arrays["decay"] = _constants()

    nc = bacc.Bacc("TRN2", target_bir_lowering=False, num_devices=1)
    args = [nc.dram_tensor(f"{n}_dram", a.shape, F32, kind="ExternalInput").ap() for n, a in arrays.items()]
    out = nc.dram_tensor("out_dram", (P, DC, S), F32, kind="ExternalOutput").ap()
    build(nc, *args, out)
    r = run_bass_kernel_spmd(nc, [{f"{n}_dram": a for n, a in arrays.items()}], core_ids=[0])
    y = np.asarray(r.results[0]["out_dram"])
    return y.transpose(1, 0, 2).reshape(D, S).T.reshape(1, S, D)
```
